# Optimizing a Trainium2 kernel written in Bass

```python
import jax, jax.numpy as jnp
from jax import lax
import numpy as np

D_MODEL = 1024
BATCH = 1
SEQ = 512
DEPTH = 2

D_MIX = D_MODEL
A_WIDTH = D_MIX // 2
B_WIDTH = D_MIX - A_WIDTH
A_HEADS = 4
A_HEAD_DIM = A_WIDTH // A_HEADS
CHUNK = 128
B_HEADS = 4
B_VAL_DIM = B_WIDTH // B_HEADS
B_KEY_DIM = B_VAL_DIM // 2
QK_WIDTH = B_HEADS * B_KEY_DIM
GATE_RANK = 16
GATE_NORMALIZER = 16.0
N_IN = 2 * A_WIDTH + 2 * QK_WIDTH + 2 * B_WIDTH + 2 * GATE_RANK
D_FF = 2816
CONV_WIDTH = 3
EPS = 1e-6

kernel_name = "hybrid_gmlp_gla_convffn_encoder"

def _split_points():
    sizes = [A_WIDTH, A_WIDTH, QK_WIDTH, QK_WIDTH, B_WIDTH, B_WIDTH, GATE_RANK, GATE_RANK]
    pts, acc = [], 0
    for s in sizes[:-1]:
        acc += s
        pts.append(acc)
    return pts

def _rmsnorm(x, g):
    xf = x.astype(jnp.float32)
    y = xf * lax.rsqrt(jnp.mean(xf * xf, axis=-1, keepdims=True) + EPS)
    return (y * g.astype(jnp.float32)).astype(x.dtype)

def _layernorm(x, g, b):
    xf = x.astype(jnp.float32)
    mu = jnp.mean(xf, axis=-1, keepdims=True)
    var = jnp.mean(jnp.square(xf - mu), axis=-1, keepdims=True)
    y = (xf - mu) * lax.rsqrt(var + EPS)
    return (y * g.astype(jnp.float32) + b.astype(jnp.float32)).astype(x.dtype)

def _spatial_gating(u, v, w_s, b_s, ln_g, ln_b):
    bsz, s = u.shape[0], u.shape[1]
    n = s // CHUNK
    vn = _layernorm(v, ln_g, ln_b).reshape(bsz, n, CHUNK, A_HEADS, A_HEAD_DIM)
    mixed = jnp.einsum('hij,bnjhd->bnihd', w_s, vn) + b_s.T[None, None, :, :, None]
    return u * mixed.reshape(bsz, s, A_HEADS, A_HEAD_DIM)

def _gla_chunked(q, k, v, log_a, include_diag):
    bsz, s, h, dk = q.shape
    dv = v.shape[-1]
    n = s // CHUNK
    f32 = jnp.float32
    qc = q.astype(f32).reshape(bsz, n, CHUNK, h, dk)
    kc = k.astype(f32).reshape(bsz, n, CHUNK, h, dk)
    vc = v.astype(f32).reshape(bsz, n, CHUNK, h, dv)
    cum = jnp.cumsum(log_a.astype(f32).reshape(bsz, n, CHUNK, h, dk), axis=2)
    cum_last = cum[:, :, -1:]
    q_dec = qc * jnp.exp(cum)
    k_inv = kc * jnp.exp(-cum)
    k_to_end = kc * jnp.exp(cum_last - cum)
    scores = jnp.einsum('bnihd,bnjhd->bnhij', q_dec, k_inv)
    mask = jnp.tril(jnp.ones((CHUNK, CHUNK), dtype=bool), k=0 if include_diag else -1)
    scores = jnp.where(mask, scores, 0.0)
    o_intra = jnp.einsum('bnhij,bnjhe->bnihe', scores, vc)
    d_state = jnp.einsum('bnjhd,bnjhe->bnhde', k_to_end, vc)
    chunk_decay = jnp.exp(cum_last[:, :, 0])

    def step(state, inp):
        ds, dec = inp
        return state * dec[..., None] + ds, state

    s0 = jnp.zeros((bsz, h, dk, dv), f32)
    _, states = lax.scan(step, s0, (jnp.swapaxes(d_state, 0, 1), jnp.swapaxes(chunk_decay, 0, 1)))
    states = jnp.swapaxes(states, 0, 1)
    o_inter = jnp.einsum('bnihd,bnhde->bnihe', q_dec, states)
    return (o_intra + o_inter).reshape(bsz, s, h, dv)

def _dwconv_centred(z, w, b):
    s = z.shape[1]
    half = CONV_WIDTH // 2
    zp = jnp.pad(z, ((0, 0), (half, half), (0, 0)))
    out = b
    for t in range(CONV_WIDTH):
        out = out + zp[:, t:t + s] * w[t]
    return out

def setup_inputs(seed: int = 0) -> dict:
    key = jax.random.key(seed)
    ks = jax.random.split(key, 20)
    f32 = jnp.float32
    nrm = lambda k, shape, scale: jax.random.normal(k, shape, f32) * scale
    return {
        "x": nrm(ks[0], (BATCH, SEQ, D_MODEL), 1.0),
        "g_mix": 1.0 + nrm(ks[1], (DEPTH, D_MODEL), 0.02),
        "w_in": nrm(ks[2], (DEPTH, D_MODEL, N_IN), D_MODEL ** -0.5),
        "w_s": nrm(ks[3], (DEPTH, A_HEADS, CHUNK, CHUNK), CHUNK ** -0.5),
        "b_s": 1.0 + nrm(ks[4], (DEPTH, A_HEADS, CHUNK), 0.1),
        "ln_g": 1.0 + nrm(ks[5], (DEPTH, A_HEADS, A_HEAD_DIM), 0.02),
        "ln_b": nrm(ks[6], (DEPTH, A_HEADS, A_HEAD_DIM), 0.02),
        "w_gate_f": nrm(ks[7], (DEPTH, GATE_RANK, QK_WIDTH), GATE_RANK ** -0.5),
        "b_gate_f": nrm(ks[8], (DEPTH, QK_WIDTH), 0.1),
        "w_gate_b": nrm(ks[9], (DEPTH, GATE_RANK, QK_WIDTH), GATE_RANK ** -0.5),
        "b_gate_b": nrm(ks[10], (DEPTH, QK_WIDTH), 0.1),
        "g_gla": 1.0 + nrm(ks[11], (DEPTH, B_HEADS, B_VAL_DIM), 0.02),
        "w_out": nrm(ks[12], (DEPTH, D_MIX, D_MODEL), D_MIX ** -0.5),
        "g_ffn": 1.0 + nrm(ks[13], (DEPTH, D_MODEL), 0.02),
        "w_up": nrm(ks[14], (DEPTH, D_MODEL, 2 * D_FF), D_MODEL ** -0.5),
        "conv_w": nrm(ks[15], (DEPTH, CONV_WIDTH, 2 * D_FF), CONV_WIDTH ** -0.5),
        "conv_b": nrm(ks[16], (DEPTH, 2 * D_FF), 0.02),
        "w_down": nrm(ks[17], (DEPTH, D_FF, D_MODEL), D_FF ** -0.5),
        "g_final": 1.0 + nrm(ks[18], (D_MODEL,), 0.02),
    }

def reference(x, g_mix, w_in, w_s, b_s, ln_g, ln_b, w_gate_f, b_gate_f, w_gate_b, b_gate_b,
              g_gla, w_out, g_ffn, w_up, conv_w, conv_b, w_down, g_final):
    bsz, s, _ = x.shape
    pts = _split_points()
    q_scale = B_KEY_DIM ** -0.5
    for l in range(DEPTH):
        h = _rmsnorm(x, g_mix[l])
        p = h @ w_in[l]
        pa_u, pa_v, pq, pk, pv, pg, r_f, r_b = jnp.split(p, pts, axis=-1)
        u = jax.nn.gelu(pa_u, approximate=False).reshape(bsz, s, A_HEADS, A_HEAD_DIM)
        va = jax.nn.gelu(pa_v, approximate=False).reshape(bsz, s, A_HEADS, A_HEAD_DIM)
        out_a = _spatial_gating(u, va, w_s[l], b_s[l], ln_g[l], ln_b[l])
        q = pq.reshape(bsz, s, B_HEADS, B_KEY_DIM) * q_scale
        k = pk.reshape(bsz, s, B_HEADS, B_KEY_DIM)
        vb = pv.reshape(bsz, s, B_HEADS, B_VAL_DIM)
        la_f = (jax.nn.log_sigmoid((r_f @ w_gate_f[l] + b_gate_f[l]).astype(jnp.float32))
                / GATE_NORMALIZER).reshape(bsz, s, B_HEADS, B_KEY_DIM)
        la_b = (jax.nn.log_sigmoid((r_b @ w_gate_b[l] + b_gate_b[l]).astype(jnp.float32))
                / GATE_NORMALIZER).reshape(bsz, s, B_HEADS, B_KEY_DIM)
        o_fwd = _gla_chunked(q, k, vb, la_f, True)
        o_bwd = jnp.flip(_gla_chunked(jnp.flip(q, 1), jnp.flip(k, 1), jnp.flip(vb, 1),
                                      jnp.flip(la_b, 1), False), 1)
        o = (o_fwd + o_bwd).astype(x.dtype)
        out_b = _rmsnorm(o, g_gla[l]) * jax.nn.silu(pg.reshape(bsz, s, B_HEADS, B_VAL_DIM))
        mixed = jnp.concatenate([out_a.reshape(bsz, s, A_WIDTH),
                                 out_b.reshape(bsz, s, B_WIDTH)], axis=-1)
        x = x + mixed @ w_out[l]
        h = _rmsnorm(x, g_ffn[l])
        z = _dwconv_centred(h @ w_up[l], conv_w[l], conv_b[l])
        z_gate, z_val = jnp.split(z, [D_FF], axis=-1)
        x = x + (jax.nn.silu(z_gate) * z_val) @ w_down[l]
    return _rmsnorm(x, g_final)


_drawn_inputs = setup_inputs


def setup_inputs(seed=0):
    import zlib

    import numpy as np

    out = dict(_drawn_inputs(seed))
    spreads = {}
    factors = {'ln_g': 4.7,
     'ln_b': 4.745,
     'b_gate_f': 3.6,
     'b_gate_b': 3.343,
     'g_gla': 5.315,
     'g_ffn': 2.988,
     'conv_b': 3.093,
     'g_final': 2.906}
    for name, (base, spread) in spreads.items():
        noise = np.random.default_rng([zlib.crc32(name.encode()), seed]).standard_normal(out[name].shape)
        drawn = base * np.exp(spread * noise) if base else spread * noise
        out[name] = __import__('jax').numpy.asarray(drawn.astype(out[name].dtype))
    for name, factor in factors.items():
        out[name] = (out[name] * factor).astype(out[name].dtype)
    return out
```

```python
from contextlib import ExitStack

import concourse.bass as bass
from concourse import mybir

F32 = mybir.dt.float32
F32R = mybir.dt.float32r
U32 = mybir.dt.uint32
ALU = mybir.AluOpType
ACT = mybir.ActivationFunctionType

P = 128
D, S, DEPTH = 1024, 512, 2
KT = D // P
CH = S // P
HEADS, DK = 4, 64
RANK = 16
DFF = 2816
FT = DFF // P
FULL_PARTS = 2
LAST_TILES = FT - FULL_PARTS * KT
EPS = 1e-6

RING = 4
SLAB = KT * P
N_K, N_Q, N_VB, N_VA, N_U, N_G, N_OUT = 0, 2, 4, 8, 12, 16, 20
N_FFN = N_OUT + KT
PART = 3 * KT
N_LAST = N_FFN + FULL_PARTS * PART
NS = N_LAST + 2 * LAST_TILES + KT
assert NS % RING == 0 and N_FFN % RING == 0 and N_LAST % RING == 0 and LAST_TILES % 2 == 0

SIDE = (["rankT", "sum", "spread"] + [f"z{t}" for t in range(4)] + [f"cum{t}" for t in range(4)]
        + [f"tail{c}" for c in range(4)] + ["keys0", "keys1"] + [f"state{s}" for s in range(3)]
        + [f"score_{d}{h}" for h in range(4) for d in "fb"] + [f"o{h}" for h in range(4)]
        + ["mix0", "mix1", "osum", "mix2", "mix3"] + [f"ospread{h}" for h in range(4)]
        + ["ffn_sum", "ffn_spread"])
NSIDE = len(SIDE)


def encoder(nc, xT, slabs, rank_w, gate_w, spatial_w, spatial_b, ln_gb, gains, gla_gain, conv, consts, outT):
    with ExitStack() as ctx:
        def sb(name, shape, dt=F32):
            return ctx.enter_context(nc.sbuf_tensor(name, shape, dt))

        def sem(name):
            return ctx.enter_context(nc.semaphore(name))

        x = sb("x", [P, KT * S])
        xg_hi = sb("xg_hi", [P, KT * S], F32R)
        xg_lo = sb("xg_lo", [P, KT * S], F32R)
        feat_hi = sb("feat_hi", [P, 4 * S], F32R)
        feat_lo = sb("feat_lo", [P, 4 * S], F32R)
        with nc.sbuf_tensor("u", [P, 4 * S], F32) as u:
            pass
        feat2_hi = sb("feat2_hi", [P, 4 * S], F32R)
        with nc.sbuf_tensor("va", [P, 4 * S], F32) as va:
            pass
        feat2_lo = sb("feat2_lo", [P, 4 * S], F32R)
        w_raw = sb("w_raw", [P, RING * SLAB])
        w_hi = sb("w_hi", [P, RING * SLAB], F32R)
        w_lo = sb("w_lo", [P, RING * SLAB], F32R)
        arena = sb("arena", [P, 23 * S])
        rstdT = sb("rstdT", [P, S])
        ssq = sb("ssq", [P, S])
        rankT = sb("rankT", [2 * RANK + 1, S])
        rank_raw = sb("rank_raw", [P, DEPTH * KT * 2 * RANK])
        RW = KT * 2 * RANK
        rank_hi = sb("rank_hi", [P, RW + P - 2 * RANK], F32R)
        rank_lo = sb("rank_lo", [P, RW + P - 2 * RANK], F32R)
        gate_sb = sb("gate_sb", [2 * RANK + 1, 4 * P])
        spatial_sb = sb("spatial_sb", [P, HEADS * P])
        spatial_b_sb = sb("spatial_b_sb", [P, HEADS * P])
        ln_sb = sb("ln_sb", [P, 2 * HEADS * P])
        gains_sb = sb("gains_sb", [P, (2 * DEPTH + 1) * KT])
        gla_sb = sb("gla_sb", [P, DEPTH * HEADS])
        conv_sb = sb("conv_sb", [P, DEPTH * FT * 8])
        consts_sb = sb("consts_sb", [P, 5 * P])
        ones = sb("ones", [P, P])
        eps = sb("eps", [P, 1])
        std = sb("std", [P, CH])
        rstd = sb("rstd", [P, CH])
        decay = sb("decay", [P, 4 * CH])
        bn = sb("bn", [P, 16 * 6])
        mv = sb("mv", [P, 16 * 2])
        ln_std = sb("ln_std", [P, 16])
        ln_rstd = sb("ln_rstd", [P, 16])
        o_std = sb("o_std", [P, 16])
        o_rstd = sb("o_rstd", [P, 16])

        ident, upto, since, after, before = (consts_sb[:, i * P:(i + 1) * P] for i in range(5))

        def slot(i, n=1):
            return arena[:, i * S:(i + n) * S]

        kT, qT = [slot(0), slot(1)], [slot(2), slot(3)]
        A = [slot(h) for h in range(4)]
        la = [slot(4 + t) for t in range(4)]
        kend = la
        osq = la
        softplus = [slot(12 + t) for t in range(4)]
        qd = [slot(8 + t) for t in range(4)]
        diag = slot(11)
        odiag = [slot(8 + h) for h in range(4)]
        ki = [slot(12 + t) for t in range(4)]
        g = ki
        sq = slot(12)
        vb = [slot(16 + t) for t in range(4)]
        mt = vb
        state = arena[:, 20 * S:23 * S].rearrange("p (s d r e) -> p s d r e", s=3, d=2, r=2)
        YW = S + 2
        y = [arena[:, i * YW:(i + 1) * YW] for i in range(4)]
        z = [arena[:, 4 * YW + i * S:4 * YW + (i + 1) * S] for i in range(4)]
        gated = [arena[:, 4 * YW + (4 + i) * S:4 * YW + (5 + i) * S] for i in range(2)]

        acc = [ctx.enter_context(nc.psum_tensor(f"acc{i}", [P, S], F32)) for i in range(RING)]
        side_banks = [ctx.enter_context(nc.psum_tensor(f"side{i}", [P, S], F32)) for i in range(RING)]
        side_at = {name: i for i, name in enumerate(SIDE)}

        def side(name):
            return side_banks[side_at[name] % RING]

        def featT(hi, k):
            if k < 4:
                return (feat_hi if hi else feat_lo)[:, k * S:(k + 1) * S]
            return (feat2_hi if hi else feat2_lo)[:, (k - 4) * S:(k - 3) * S]

        def xg_out(m):
            return slot(12 + m)

        x_loaded = [sem(f"x_loaded{i}") for i in range(4)]
        gains_loaded, vec_loaded, par_loaded = sem("gains_loaded"), sem("vec_loaded"), sem("par_loaded")
        raw_loaded = [sem(f"raw_loaded{i}") for i in range(RING)]
        hi_done, lo_done = sem("hi_done"), sem("lo_done")
        group_used = sem("group_used")
        acc_ready = sem("acc_ready")
        side_ready = sem("side_ready")
        setup_done = sem("setup_done")
        rank_hi_done, rank_lo_done = sem("rank_hi_done"), sem("rank_lo_done")
        xg_hi_done, xg_ready = sem("xg_hi_done"), sem("xg_ready")
        sq_done, ssq_added = sem("sq_done"), sem("ssq_added")
        std_done, rstd_done = sem("std_done"), sem("rstd_done")
        diag_done, rstdT_done = sem("diag_done"), sem("rstdT_done")
        kT_done, qT_done = sem("kT_done"), sem("qT_done")
        rankT_done = sem("rankT_done")
        softplus_done, la_done = sem("softplus_done"), sem("la_done")
        cum_exp_done = sem("cum_exp_done")
        qk_done = sem("qk_done")
        vb_done = sem("vb_done")
        tail_done, kend_done = sem("tail_done"), sem("kend_done")
        state_done = sem("state_done")
        va_gelu = sem("va_gelu")
        bn_done, mv_done = sem("bn_done"), sem("mv_done")
        ln_std_done, ln_rstd_done = sem("ln_std_done"), sem("ln_rstd_done")
        vhat_done, vn_done = sem("vhat_done"), sem("vn_done")
        u_lin, u_gelu = sem("u_lin"), sem("u_gelu")
        score_copied, score_done = sem("score_copied"), sem("score_done")
        osq_done, og_done = sem("osq_done"), sem("og_done")
        g_lin, g_silu = sem("g_lin"), sem("g_silu")
        mixed, u_mixed = sem("mixed"), sem("u_mixed")
        o_std_done, o_rstd_done, odiag_done = sem("o_std_done"), sem("o_rstd_done"), sem("odiag_done")
        o_normed, o_gated = sem("o_normed"), sem("o_gated")
        feat_hi_done, feat_ready = sem("feat_hi_done"), sem("feat_ready")
        x_done = sem("x_done")
        halo = sem("halo")
        y_ready, centre_done, taps_done = sem("y_ready"), sem("centre_done"), sem("taps_done")
        silu_done, gated_done = sem("silu_done"), sem("gated_done")
        final_done, out_stored = sem("final_done"), sem("out_stored")
        waits_passed = sem("waits_passed")
        NF = KT + FT
        NX = 4 * KT
        NY = 2 * FT

        def on_its_own(eng):
            eng.sem_inc(waits_passed, 1)

        block = ctx.enter_context(nc.Block())

        @block.sync
        def _(sp):
            def load_slab(L, q, j):
                sp.wait_ge(lo_done, L * NS + q * RING + (j + 1))
                sp.dma_start(w_raw[:, j * SLAB:(j + 1) * SLAB],
                             slabs[bass.ds(L * NS + q * RING + j, 1), :, :].rearrange("o p n -> (o p) n")
                             ).then_inc(raw_loaded[j], 16)

            with sp.Fori(0, DEPTH) as L:
                for j in range(RING):
                    load_slab(L, 0, j)
                for dst, src in (
                        (gate_sb[:, :], gate_w[bass.ds(L, 1), :, :].rearrange("o p n -> (o p) n")),
                        (spatial_sb[:, :], spatial_w[bass.ds(L, 1), :, :].rearrange("o p n -> (o p) n")),
                        (spatial_b_sb[:, :], spatial_b[bass.ds(L, 1), :].broadcast_to([P, HEADS * P])),
                        (ln_sb[:, :], ln_gb[bass.ds(L, 1), :].broadcast_to([P, 2 * HEADS * P]))):
                    sp.dma_start(dst, src).then_inc(par_loaded, 16)
                with sp.Fori(1, NS // RING) as q:
                    for j in range(RING):
                        load_slab(L, q, j)
            for m in range(KT):
                sp.wait_ge(final_done, m + 1)
                sp.dma_start(outT[m * P:(m + 1) * P, :], xg_out(m)).then_inc(out_stored, 16)
            sp.wait_ge(out_stored, 16 * KT)

        @block.gpsimd
        def _(pool):
            pool.memset(ones[:, :], 1.0).then_inc(setup_done, 1)
            for part in (rank_hi, rank_lo):
                pool.memset(part[:, RW:RW + P - 2 * RANK].bitcast(F32), 0.0).then_inc(setup_done, 1)
            pool.memset(eps[:, :], EPS).then_inc(lo_done, RING)
            with pool.Fori(0, DEPTH * NS // RING) as q:
                for j in range(RING):
                    w = slice(j * SLAB, (j + 1) * SLAB)
                    pool.wait_ge(hi_done, q * RING + (j + 1))
                    pool.tensor_tensor(w_lo[:, w], w_raw[:, w], w_hi[:, w].bitcast(F32),
                                       ALU.subtract).then_inc(lo_done, 1)

        @block.scalar
        def _(act):
            def split_hi(n, j):
                w = slice(j * SLAB, (j + 1) * SLAB)
                act.activation(w_hi[:, w], w_raw[:, w], ACT.Copy).then_inc(hi_done, 1)

            def split_after(L, n):
                j = n % RING if isinstance(n, int) else None
                split_next(L, n, j)

            def split_next(L, n, j):
                act.wait_ge(raw_loaded[j], 16 * (L * (NS // RING)) + 16 * (n // RING + 2))
                split_hi(n, j)

            def gain_hi(m, r):
                act.activation(xg_hi[:, bass.ds(m * S, S)], x[:, bass.ds(m * S, S)], ACT.Copy,
                               scale=gains_sb[:, bass.ds(r * KT + m, 1)]).then_inc(xg_hi_done, 1)

            def square(m, r):
                act.wait_ge(ssq_added, r * (KT + 1) + m + 1)
                on_its_own(act)
                act.activation(sq, x[:, bass.ds(m * S, S)], ACT.Square).then_inc(sq_done, 1)

            def emit(m, r, x_count):
                act.wait_ge(*x_count)
                on_its_own(act)
                gain_hi(m, r)
                square(m, r)

            def root(L, name, done, count, r_ap, scale, n):
                act.wait_ge(side_ready, count)
                act.activation(r_ap, side(name)[:, 0:n], ACT.Sqrt, bias=eps[:, 0:1], scale=scale).then_inc(done, 1)

            act.dma_start(gains_sb[:, :], gains).then_inc(gains_loaded, 16)
            for c in range(4):
                rows = xT[c * 2 * P:(c + 1) * 2 * P, :].rearrange("(k p) s -> p k s", p=P)
                act.dma_start(x[:, c * 2 * S:(c + 1) * 2 * S].rearrange("p (k s) -> p k s", k=2),
                              rows).then_inc(x_loaded[c], 16)
            act.dma_start(consts_sb[:, :], consts).then_inc(vec_loaded, 16)
            act.dma_start(rank_raw[:, :], rank_w).then_inc(vec_loaded, 16)
            act.dma_start(gla_sb[:, :], gla_gain).then_inc(vec_loaded, 16)
            act.dma_start(conv_sb[:, :], conv).then_inc(vec_loaded, 16)
            act.wait_ge(gains_loaded, 16)
            for m in range(KT):
                act.wait_ge(x_loaded[m // 2], 16)
                gain_hi(m, 0)
                if m % 2 == 0:
                    act.wait_ge(raw_loaded[m // 2], 16)
                    split_hi(m // 2, m // 2)
            for m in range(KT):
                square(m, 0)

            with act.Fori(0, DEPTH) as L:
                def acc_at(n):
                    act.wait_ge(acc_ready, L * NS + n)

                def side_wait(name):
                    act.wait_ge(side_ready, L * NSIDE + (side_at[name] + 1))

                act.wait_ge(vec_loaded, 16 * 4)
                act.activation(rank_hi[:, 0:RW], rank_raw[:, bass.ds(L * RW, RW)],
                               ACT.Copy).then_inc(rank_hi_done, 1)
                acc_at(1)
                split_after(L, 0)
                root(L, "sum", std_done, L * NSIDE + 2, std[:, :], 1.0 / D, CH)
                acc_at(2)
                split_after(L, 1)
                side_wait("spread")
                act.activation(rstdT[:, :], side("spread")[:, :], ACT.Copy).then_inc(rstdT_done, 1)
                acc_at(3)
                split_after(L, 2)
                for t in range(CH):
                    side_wait(f"z{t}")
                    act.activation(softplus[t], side(f"z{t}")[:, :], ACT.Abs).then_inc(softplus_done, 1)
                    act.wait_ge(softplus_done, L * 12 + (2 * t + 1))
                    act.activation(softplus[t], softplus[t], ACT.Exp, scale=-1.0).then_inc(softplus_done, 1)
                acc_at(4)
                split_after(L, 3)
                for t in range(CH):
                    act.wait_ge(softplus_done, L * 12 + (2 * t + 2))
                    act.activation(softplus[t], softplus[t], ACT.Ln, bias=ones[:, 0:1]).then_inc(softplus_done, 1)
                act.wait_ge(group_used, L * 6 + 1)
                split_after(L, 4)
                act.wait_ge(group_used, L * 6 + 2)
                split_after(L, 5)
                for t in range(4):
                    side_wait(f"cum{t}")
                    cum = side(f"cum{t}")
                    act.wait_ge(la_done, L * 4 + 4)
                    act.activation(qd[t], cum[:, :], ACT.Exp, scale=1.0 / 16).then_inc(cum_exp_done, 1)
                    act.activation(ki[t], cum[:, :], ACT.Exp, scale=-1.0 / 16).then_inc(cum_exp_done, 1)
                    edge = P - 1 if t < 2 else 0
                    act.activation(decay[:, t * CH:(t + 1) * CH],
                                   cum[:, :].rearrange("p (c i) -> p c i", c=CH)[:, :, edge],
                                   ACT.Exp, scale=1.0 / 16).then_inc(cum_exp_done, 1)
                act.wait_ge(group_used, L * 6 + 3)
                split_after(L, 6)
                for t in range(CH):
                    acc_at(N_VB + t + 1)
                    if t == CH - 1:
                        split_after(L, 7)
                    act.activation(vb[t], acc[t][:, :], ACT.Copy, scale=rstd[:, t:t + 1]).then_inc(vb_done, 1)
                for c in range(CH):
                    side_wait(f"tail{c}")
                    act.activation(kend[c], side(f"tail{c}")[:, :], ACT.Exp, scale=1.0 / 16).then_inc(tail_done, 1)
                act.wait_ge(group_used, L * 6 + 4)
                split_after(L, 8)
                act.wait_ge(group_used, L * 6 + 5)
                split_after(L, 9)
                act.wait_ge(group_used, L * 6 + 6)
                split_after(L, 10)
                for t in range(CH):
                    acc_at(N_VA + t + 1)
                    if t == CH - 1:
                        split_after(L, 11)
                    act.activation(va[:, t * S:(t + 1) * S], acc[t][:, :], ACT.Gelu,
                                   scale=rstd[:, t:t + 1]).then_inc(va_gelu, 1)

                def copy_score(h):
                    side_wait(f"score_f{h}")
                    act.activation(A[h], side(f"score_f{h}")[:, :], ACT.Copy).then_inc(score_copied, 1)

                def gelu_u(h):
                    act.wait_ge(u_lin, L * 4 + (h + 1))
                    uh = u[:, h * S:(h + 1) * S]
                    act.activation(uh, uh, ACT.Gelu).then_inc(u_gelu, 1)

                def square_o(h):
                    side_wait(f"o{h}")
                    act.activation(osq[h], side(f"o{h}")[:, :], ACT.Square).then_inc(osq_done, 1)

                acc_at(N_U + 1)
                split_after(L, 12)
                copy_score(0)
                act.wait_ge(mv_done, L * 16 + 16)
                act.activation(ln_std[:, :], mv[:, :].rearrange("p (a b) -> p a b", b=2)[:, :, 1], ACT.Sqrt,
                               bias=eps[:, 0:1]).then_inc(ln_std_done, 1)
                gelu_u(0)
                acc_at(N_U + 2)
                split_after(L, 13)
                copy_score(1)
                copy_score(2)
                gelu_u(1)
                acc_at(N_U + 3)
                split_after(L, 14)
                copy_score(3)
                gelu_u(2)
                square_o(0)
                acc_at(N_U + 4)
                split_after(L, 15)
                gelu_u(3)
                square_o(1)
                square_o(2)
                square_o(3)

                def hi_of(count, src, k):
                    act.wait_ge(*count)
                    act.activation(featT(True, k), src, ACT.Copy).then_inc(feat_hi_done, 1)

                def silu_g(h):
                    act.wait_ge(g_lin, L * 4 + (h + 1))
                    act.activation(g[h], g[h], ACT.Silu).then_inc(g_silu, 1)

                acc_at(N_G + 1)
                split_after(L, 16)
                hi_of((u_mixed, L * 4 + 1), mt[0], 0)
                hi_of((u_mixed, L * 4 + 2), mt[1], 1)
                acc_at(N_G + 2)
                split_after(L, 17)
                root(L, "osum", o_std_done, L * NSIDE + (side_at["osum"] + 1), o_std[:, :], 1.0 / P, 16)
                hi_of((u_mixed, L * 4 + 3), mt[2], 2)
                hi_of((u_mixed, L * 4 + 4), mt[3], 3)
                acc_at(N_G + 3)
                split_after(L, 18)
                silu_g(0)
                silu_g(1)
                hi_of((o_gated, L * 4 + 1), mt[0], 4)
                silu_g(2)
                acc_at(N_G + 4)
                split_after(L, 19)
                hi_of((o_gated, L * 4 + 2), mt[1], 5)
                silu_g(3)
                hi_of((o_gated, L * 4 + 3), mt[2], 6)
                hi_of((o_gated, L * 4 + 4), mt[3], 7)

                with act.Fori(0, KT // RING) as q:
                    for j in range(RING):
                        m = q * RING + j
                        act.wait_ge(acc_ready, L * NS + q * RING + (N_OUT + j + 1))
                        act.wait_ge(raw_loaded[j], 16 * (L * (NS // RING)) + 16 * q + 16 * (N_OUT // RING + 2))
                        split_hi(None, j)
                        emit(m, L * 2 + 1, (x_done, L * NX + m + (1 + RING)))

                root(L, "ffn_sum", std_done, L * NSIDE + (side_at["ffn_sum"] + 1), std[:, :], 1.0 / D, CH)
                side_wait("ffn_spread")
                act.activation(rstdT[:, :], side("ffn_spread")[:, :], ACT.Copy).then_inc(rstdT_done, 1)

                def up_quad(slab, tile, feat):
                    for b in range(2):
                        f = L * FT + tile + b
                        for v in range(2):
                            j = 2 * b + v
                            coef = (f * 2 + v) * 4
                            act.wait_ge(y_ready, f * 2 + v + 1)
                            on_its_own(act)
                            act.activation(z[j], y[j][:, 1:S + 1], ACT.Identity,
                                           scale=conv_sb[:, bass.ds(coef + 1, 1)],
                                           bias=conv_sb[:, bass.ds(coef + 3, 1)]).then_inc(centre_done, 1)
                            act.wait_ge(raw_loaded[j], 16 * (L * (NS // RING)) + 4 * slab + 32)
                            split_hi(None, j)
                            if v == 0:
                                act.wait_ge(taps_done, f * 4 + 2)
                                act.activation(z[j], z[j], ACT.Silu).then_inc(silu_done, 1)
                        act.wait_ge(gated_done, f + 1)
                        on_its_own(act)
                        act.activation(feat(b), gated[b], ACT.Copy).then_inc(feat_hi_done, 1)

                def down(slab, step, last):
                    with act.Fori(0, KT // RING) as q:
                        for j in range(RING):
                            m = q * RING + j
                            act.wait_ge(acc_ready, L * NS + slab + q * RING + (j + 1))
                            if not last:
                                act.wait_ge(raw_loaded[j], 16 * (L * (NS // RING)) + 4 * slab + 16 * q + 32)
                                split_hi(None, j)
                            else:
                                with act.If(L * NS + q * RING + (slab + j + RING) < DEPTH * NS):
                                    act.wait_ge(raw_loaded[j], 16 * (L * (NS // RING)) + 4 * slab + 16 * q + 32)
                                    split_hi(None, j)
                                emit(m, L * 2 + 2, (x_done, L * NX + m + (NX - KT + 1 + RING)))

                with act.Fori(0, FULL_PARTS) as part:
                    for half, dst in ((0, feat_hi), (1, feat2_hi)):
                        with act.Fori(0, 2) as q:
                            up_quad(part * PART + q * RING + (N_FFN + half * 8), part * KT + q * 2 + half * 4,
                                    lambda b: dst[:, bass.ds(q * (2 * S) + b * S, S)])
                    down(part * PART + (N_FFN + 2 * KT), None, False)
                for q in range(LAST_TILES // 2):
                    up_quad(N_LAST + q * RING, FULL_PARTS * KT + 2 * q, lambda b: featT(True, 2 * q + b))
                down(N_LAST + 2 * LAST_TILES, None, True)

            root(DEPTH, "sum", std_done, DEPTH * NSIDE + 1, std[:, :], 1.0 / D, CH)
            act.wait_ge(side_ready, DEPTH * NSIDE + 2)
            act.activation(rstdT[:, :], side("spread")[:, :], ACT.Copy).then_inc(rstdT_done, 1)

        @block.vector
        def _(dve):
            def gain_lo(m, r):
                w = bass.ds(m * S, S)
                dve.wait_ge(xg_hi_done, r * KT + m + 1)
                dve.scalar_tensor_tensor(out=xg_lo[:, w], in0=x[:, w], scalar=gains_sb[:, bass.ds(r * KT + m, 1)],
                                         in1=xg_hi[:, w].bitcast(F32), op0=ALU.mult,
                                         op1=ALU.subtract).then_inc(xg_ready, 1)

            def add_square(m, r):
                dve.wait_ge(sq_done, r * KT + m + 1)
                dve.wait_ge(ssq_added, r * (KT + 1) + m + 1)
                dve.tensor_tensor(ssq[:, :], ssq[:, :], sq, ALU.add).then_inc(ssq_added, 1)

            def emit(m, r):
                gain_lo(m, r)
                add_square(m, r)

            def token_scale(r):
                dve.wait_ge(std_done, r + 1)
                dve.reciprocal(rstd[:, :], std[:, :]).then_inc(rstd_done, 1)
                dve.wait_ge(rstd_done, r + 1)
                dve.tensor_tensor(diag.rearrange("p (c i) -> p c i", c=CH),
                                  ident.unsqueeze(1).broadcast_to([P, CH, P]),
                                  rstd[:, :].unsqueeze(2).broadcast_to([P, CH, P]), ALU.mult).then_inc(diag_done, 1)
                dve.memset(ssq[:, :], 0.0).then_inc(ssq_added, 1)

            dve.memset(ssq[:, :], 0.0).then_inc(ssq_added, 1)
            dve.memset(rankT[2 * RANK:2 * RANK + 1, :], 1.0).then_inc(setup_done, 1)
            dve.sem_inc(x_done, RING)
            dve.wait_ge(gains_loaded, 16)
            for m in range(KT):
                gain_lo(m, 0)
            for m in range(KT):
                add_square(m, 0)

            with dve.Fori(0, DEPTH) as L:
                def acc_at(n):
                    dve.wait_ge(acc_ready, L * NS + n)

                def side_wait(name):
                    dve.wait_ge(side_ready, L * NSIDE + (side_at[name] + 1))

                dve.wait_ge(rank_hi_done, L + 1)
                dve.tensor_tensor(rank_lo[:, 0:RW], rank_raw[:, bass.ds(L * RW, RW)],
                                  rank_hi[:, 0:RW].bitcast(F32), ALU.subtract).then_inc(rank_lo_done, 1)
                token_scale(L * 2)
                dve.wait_ge(rstdT_done, L * 2 + 1)
                side_wait("rankT")
                dve.tensor_tensor(rankT[0:2 * RANK, :], side("rankT")[0:2 * RANK, :], rstdT[0:2 * RANK, :],
                                  ALU.mult).then_inc(rankT_done, 1)
                for t in range(2):
                    acc_at(N_K + t + 1)
                    dve.tensor_tensor(kT[t], acc[t][:, :], rstdT[:, :], ALU.mult).then_inc(kT_done, 1)
                for t in range(2):
                    acc_at(N_Q + t + 1)
                    dve.scalar_tensor_tensor(out=qT[t], in0=acc[2 + t][:, :], scalar=DK ** -0.5, in1=rstdT[:, :],
                                             op0=ALU.mult, op1=ALU.mult).then_inc(qT_done, 1)
                for t in range(CH):
                    dve.wait_ge(softplus_done, L * 12 + (8 + t + 1))
                    dve.scalar_tensor_tensor(out=la[t], in0=side(f"z{t}")[:, :], scalar=0.0, in1=softplus[t],
                                             op0=ALU.min, op1=ALU.subtract).then_inc(la_done, 1)
                dve.wait_ge(qT_done, L * 2 + 2)
                for t in range(4):
                    dve.wait_ge(cum_exp_done, L * 12 + (3 * t + 2))
                    dve.tensor_tensor(qd[t], qd[t], qT[t % 2], ALU.mult).then_inc(qk_done, 1)
                    dve.tensor_tensor(ki[t], ki[t], kT[t % 2], ALU.mult).then_inc(qk_done, 1)
                for c in range(CH):
                    side_wait(f"keys{c // 2}")
                    dve.wait_ge(tail_done, L * 4 + (c + 1))
                    ke = kend[c].rearrange("p (d n) -> p d n", d=2)
                    keys = side(f"keys{c // 2}")[:, (c % 2) * 256:(c % 2 + 1) * 256]
                    dve.tensor_tensor(ke, ke, keys.unsqueeze(1).broadcast_to([P, 2, 256]),
                                      ALU.mult).then_inc(kend_done, 1)
                side_wait("state0")
                dve.wait_ge(cum_exp_done, L * 12 + 12)
                dve.tensor_copy(state[:, 0, :, :, :].rearrange("p d r e -> p (d r e)"),
                                side("state0")[:, :]).then_inc(state_done, 1)
                for s in range(1, 3):
                    side_wait(f"state{s}")
                    dve.wait_ge(state_done, L * 9 + (1 + 4 * (s - 1)))
                    for dr in range(4):
                        chunk = s if dr < 2 else CH - 1 - s
                        dve.scalar_tensor_tensor(out=state[:, s, dr // 2, dr % 2, :],
                                                 in0=state[:, s - 1, dr // 2, dr % 2, :],
                                                 scalar=decay[:, dr * CH + chunk:dr * CH + chunk + 1],
                                                 in1=side(f"state{s}")[:, dr * P:(dr + 1) * P],
                                                 op0=ALU.mult, op1=ALU.add).then_inc(state_done, 1)
                for t in range(CH):
                    dve.wait_ge(va_gelu, L * 4 + (t + 1))
                    for h in range(HEADS):
                        i = t * HEADS + h
                        dve.bn_stats(bn[:, i * 6:(i + 1) * 6], va[:, i * P:(i + 1) * P]).then_inc(bn_done, 1)
                    for h in range(HEADS):
                        i = t * HEADS + h
                        dve.wait_ge(bn_done, L * 16 + (i + 1))
                        on_its_own(dve)
                        dve.bn_aggr(mv[:, i * 2:(i + 1) * 2], bn[:, i * 6:(i + 1) * 6]).then_inc(mv_done, 1)

                def scale_u(h):
                    acc_at(N_U + h + 1)
                    dve.tensor_tensor(u[:, h * S:(h + 1) * S], acc[h][:, :], rstdT[:, :], ALU.mult).then_inc(u_lin, 1)

                def select_scores(h):
                    side_wait(f"score_b{h}")
                    dve.wait_ge(score_copied, L * 4 + (h + 1))
                    on_its_own(dve)
                    dve.copy_predicated(A[h].rearrange("p (c i) -> p c i", c=CH),
                                        after.bitcast(U32).unsqueeze(1).broadcast_to([P, CH, P]),
                                        side(f"score_b{h}")[:, :].rearrange("p (c i) -> p c i", c=CH)
                                        ).then_inc(score_done, 1)

                def layernorm(t):
                    for h in range(HEADS):
                        i = t * HEADS + h
                        vi = va[:, i * P:(i + 1) * P]
                        dve.tensor_scalar(vi, vi, mv[:, i * 2:i * 2 + 1], ln_rstd[:, i:i + 1],
                                          ALU.subtract, ALU.mult).then_inc(vhat_done, 1)
                    vt = va[:, t * S:(t + 1) * S]
                    dve.wait_ge(vhat_done, L * 16 + 4 * (t + 1))
                    dve.tensor_tensor(vt, vt, ln_sb[:, 0:S], ALU.mult).then_inc(vn_done, 1)
                    dve.wait_ge(vn_done, L * 8 + (2 * t + 1))
                    dve.tensor_tensor(vt, vt, ln_sb[:, S:2 * S], ALU.add).then_inc(vn_done, 1)

                def gain_o(h):
                    dve.wait_ge(osq_done, L * 4 + (h + 1))
                    dve.tensor_scalar(A[h], side(f"o{h}")[:, :], gla_sb[:, bass.ds(L * HEADS + h, 1)], None,
                                      ALU.mult).then_inc(og_done, 1)

                scale_u(0)
                select_scores(0)
                dve.wait_ge(ln_std_done, L + 1)
                dve.reciprocal(ln_rstd[:, :], ln_std[:, :]).then_inc(ln_rstd_done, 1)
                dve.wait_ge(ln_rstd_done, L + 1)
                dve.wait_ge(par_loaded, L * 64 + 64)
                layernorm(0)
                scale_u(1)
                select_scores(1)
                select_scores(2)
                layernorm(1)
                scale_u(2)
                select_scores(3)
                layernorm(2)
                gain_o(0)
                scale_u(3)
                layernorm(3)
                for h in range(1, HEADS):
                    gain_o(h)

                def scale_g(h):
                    acc_at(N_G + h + 1)
                    dve.tensor_tensor(g[h], acc[h][:, :], rstdT[:, :], ALU.mult).then_inc(g_lin, 1)

                def mix(h):
                    side_wait(f"mix{h}")
                    dve.tensor_tensor(mt[h].rearrange("p (c i) -> p c i", c=CH),
                                      side(f"mix{h}")[:, :].rearrange("p (c i) -> p c i", c=CH),
                                      spatial_b_sb[:, h * P:(h + 1) * P].unsqueeze(1).broadcast_to([P, CH, P]),
                                      ALU.add).then_inc(mixed, 1)
                    dve.wait_ge(mixed, L * 4 + (h + 1))
                    dve.wait_ge(u_gelu, L * 4 + (h + 1))
                    dve.tensor_tensor(mt[h], mt[h], u[:, h * S:(h + 1) * S], ALU.mult).then_inc(u_mixed, 1)

                def lo_of(src, k):
                    dve.wait_ge(feat_hi_done, L * NF + (k + 1))
                    dve.tensor_tensor(featT(False, k), src, featT(True, k).bitcast(F32),
                                      ALU.subtract).then_inc(feat_ready, 1)

                def diagonal_o(h):
                    dve.tensor_tensor(odiag[h].rearrange("p (c i) -> p c i", c=CH),
                                      ident.unsqueeze(1).broadcast_to([P, CH, P]),
                                      o_rstd[:, h * CH:(h + 1) * CH].unsqueeze(2).broadcast_to([P, CH, P]),
                                      ALU.mult).then_inc(odiag_done, 1)

                def norm_o(h):
                    side_wait(f"ospread{h}")
                    dve.wait_ge(og_done, L * 4 + (h + 1))
                    dve.tensor_tensor(mt[h], A[h], side(f"ospread{h}")[:, :], ALU.mult).then_inc(o_normed, 1)
                    dve.wait_ge(o_normed, L * 4 + (h + 1))
                    dve.wait_ge(g_silu, L * 4 + (h + 1))
                    dve.tensor_tensor(mt[h], mt[h], g[h], ALU.mult).then_inc(o_gated, 1)

                scale_g(0)
                mix(0)
                mix(1)
                lo_of(mt[0], 0)
                lo_of(mt[1], 1)
                scale_g(1)
                dve.wait_ge(o_std_done, L + 1)
                dve.reciprocal(o_rstd[:, :], o_std[:, :]).then_inc(o_rstd_done, 1)
                dve.wait_ge(o_rstd_done, L + 1)
                for h in range(HEADS):
                    diagonal_o(h)
                mix(2)
                mix(3)
                lo_of(mt[2], 2)
                lo_of(mt[3], 3)
                scale_g(2)
                norm_o(0)
                lo_of(mt[0], 4)
                norm_o(1)
                scale_g(3)
                lo_of(mt[1], 5)
                norm_o(2)
                norm_o(3)
                lo_of(mt[2], 6)
                lo_of(mt[3], 7)

                def add_to_x(n, m, j, count):
                    dve.wait_ge(acc_ready, n + 1)
                    dve.tensor_tensor(x[:, bass.ds(m * S, S)], x[:, bass.ds(m * S, S)], acc[j][:, :],
                                      ALU.add).then_inc(x_done, 1)

                with dve.Fori(0, KT // RING) as q:
                    for j in range(RING):
                        m = q * RING + j
                        add_to_x(L * NS + m + N_OUT, m, j, None)
                        emit(m, L * 2 + 1)
                token_scale(L * 2 + 1)
                for i in range(4):
                    for edge in (0, S + 1):
                        dve.memset(y[i][:, edge:edge + 1], 0.0).then_inc(halo, 1)
                dve.wait_ge(halo, L * 8 + 8)
                dve.wait_ge(rstdT_done, L * 2 + 2)
                on_its_own(dve)

                def up_quad(slab, tile, feat, feat_lo_of):
                    def low_part(b):
                        dve.wait_ge(feat_hi_done, L * NF + tile + (b + KT + 1))
                        dve.tensor_tensor(feat_lo_of(b), gated[b], feat(b).bitcast(F32),
                                          ALU.subtract).then_inc(feat_ready, 1)

                    for b in range(2):
                        f = L * FT + tile + b
                        for v in range(2):
                            j = 2 * b + v
                            coef = (f * 2 + v) * 4
                            dve.wait_ge(acc_ready, L * NS + slab + (j + 1))
                            dve.tensor_tensor(y[j][:, 1:S + 1], acc[j][:, :], rstdT[:, :],
                                              ALU.mult).then_inc(y_ready, 1)
                            if b == 1 and v == 0:
                                low_part(0)
                            dve.wait_ge(centre_done, f * 2 + v + 1)
                            for tap in (0, 2):
                                dve.scalar_tensor_tensor(out=z[j], in0=y[j][:, tap:tap + S],
                                                         scalar=conv_sb[:, bass.ds(coef + tap, 1)], in1=z[j],
                                                         op0=ALU.mult, op1=ALU.add).then_inc(taps_done, 1)
                                dve.wait_ge(taps_done, f * 4 + (2 * v + tap // 2 + 1))
                        dve.wait_ge(silu_done, f + 1)
                        dve.tensor_tensor(gated[b], z[2 * b], z[2 * b + 1], ALU.mult).then_inc(gated_done, 1)
                    low_part(1)

                with dve.Fori(0, FULL_PARTS) as part:
                    for half, hi, lo in ((0, feat_hi, feat_lo), (1, feat2_hi, feat2_lo)):
                        with dve.Fori(0, 2) as q:
                            up_quad(part * PART + q * RING + (N_FFN + half * 8), part * KT + q * 2 + half * 4,
                                    lambda b: hi[:, bass.ds(q * (2 * S) + b * S, S)],
                                    lambda b: lo[:, bass.ds(q * (2 * S) + b * S, S)])
                    with dve.Fori(0, KT // RING) as q:
                        for j in range(RING):
                            add_to_x(L * NS + part * PART + q * RING + (N_FFN + 2 * KT + j), q * RING + j, j, None)
                for q in range(LAST_TILES // 2):
                    up_quad(N_LAST + q * RING, FULL_PARTS * KT + 2 * q, lambda b: featT(True, 2 * q + b),
                            lambda b: featT(False, 2 * q + b))
                with dve.Fori(0, KT // RING) as q:
                    for j in range(RING):
                        m = q * RING + j
                        add_to_x(L * NS + m + (N_LAST + 2 * LAST_TILES), m, j, None)
                        emit(m, L * 2 + 2)

            token_scale(2 * DEPTH)
            dve.wait_ge(rstdT_done, 2 * DEPTH + 1)
            for m in range(KT):
                col = 2 * DEPTH * KT + m
                dve.scalar_tensor_tensor(out=xg_out(m), in0=x[:, m * S:(m + 1) * S],
                                         scalar=gains_sb[:, col:col + 1], in1=rstdT[:, :],
                                         op0=ALU.mult, op1=ALU.mult).then_inc(final_done, 1)

        @block.tensor
        def _(pe):
            def three(out, w_pair, a_pair, first, last):
                (wh, wl), (ah, al) = w_pair, a_pair
                pe.matmul(out, wh, ah, start=first, stop=False)
                pe.matmul(out, wh, al, start=False, stop=False)
                return pe.matmul(out, wl, ah, start=False, stop=last)

            def w_block(j, at, n=P):
                a = j * SLAB + at
                return w_hi[:, a:a + n], w_lo[:, a:a + n]

            def xg(k, a=0, n=S):
                return xg_hi[:, k * S + a:k * S + a + n], xg_lo[:, k * S + a:k * S + a + n]

            def feat(k):
                return featT(True, k), featT(False, k)

            def project(j, source, blocks=KT, ready=None):
                for k in range(blocks):
                    if ready is not None:
                        pe.wait_ge(ready[0], ready[1] + (k + 1))
                    last = three(acc[j][:, :], w_block(j, k * P), source(k), k == 0, k == blocks - 1)
                last.then_inc(acc_ready, 1)

            def project_pair(source, blocks, ready):
                for k, j in [(k, j) for j in range(2) for k in range(blocks - 1)] + [(blocks - 1, 0), (blocks - 1, 1)]:
                    if j == 0:
                        pe.wait_ge(ready[0], ready[1] + (k + 1))
                    last = three(acc[j][:, :], w_block(j, k * P), source(k), k == 0, k == blocks - 1)
                    if k == blocks - 1:
                        last.then_inc(acc_ready, 1)

            def token_sums(name, r):
                pe.wait_ge(ssq_added, (r + 1) * (KT + 1))
                for c in range(CH):
                    last = pe.matmul(side(name)[:, c:c + 1], ssq[:, c * P:(c + 1) * P], ones[:, 0:1],
                                     start=True, stop=True)
                last.then_inc(side_ready, 1)

            def spread(name, d):
                pe.matmul(side(name)[:, :], ones[:, :], d, start=True, stop=True).then_inc(side_ready, 1)

            pe.wait_ge(setup_done, 4)

            with pe.Fori(0, DEPTH) as L:
                def slab_wait(n):
                    pe.wait_ge(lo_done, L * NS + (n + 1 + RING))

                slab_wait(0)
                pe.wait_ge(x_done, L * NX + 1)
                project(0, xg, ready=(xg_ready, L * 16))
                pe.wait_ge(rank_lo_done, L + 1)
                for k in range(KT):
                    w = [part[:, k * 2 * RANK:k * 2 * RANK + P] for part in (rank_hi, rank_lo)]
                    last = three(side("rankT")[:, :], w, xg(k), k == 0, k == KT - 1)
                last.then_inc(side_ready, 1)
                token_sums("sum", L * 2)
                slab_wait(1)
                project(1, xg)
                pe.wait_ge(diag_done, L * 2 + 1)
                spread("spread", diag)
                slab_wait(2)
                project(2, xg)
                pe.wait_ge(rankT_done, L + 1)
                pe.wait_ge(par_loaded, L * 64 + 64)
                for t in range(CH):
                    pe.matmul(side(f"z{t}")[:, :], rankT[:, t * P:(t + 1) * P], gate_sb[:, :],
                              start=True, stop=True).then_inc(side_ready, 1)

                slab_wait(3)
                project(3, xg)

                def token_major(n0, s, bank_free):
                    slab_wait(n0 + s)
                    for kk in range(2):
                        k = 2 * s + kk
                        for t in range(CH):
                            if k == 0:
                                pe.wait_ge(*bank_free(t))
                            (wh, wl), (ah, al) = w_block(s, kk * S, S), xg(k, t * P, P)
                            pe.matmul(acc[t][:, :], ah, wh, start=(k == 0), stop=False)
                            pe.matmul(acc[t][:, :], al, wh, start=False, stop=False)
                            last = pe.matmul(acc[t][:, :], ah, wl, start=False, stop=(k == KT - 1))
                            if k == KT - 1:
                                last.then_inc(acc_ready, 1)
                    if s < 3:
                        last.then_inc(group_used, 1)

                def vb_bank(t):
                    return (kT_done, L * 2 + (t + 1)) if t < 2 else (qT_done, L * 2 + (t - 1))

                token_major(N_VB, 0, vb_bank)
                token_major(N_VB, 1, vb_bank)
                for dt in range(4):
                    pe.wait_ge(la_done, L * 4 + 4)
                    for c in range(CH):
                        last = pe.matmul(side(f"cum{dt}")[:, c * P:(c + 1) * P], la[c][:, dt * P:(dt + 1) * P],
                                         upto if dt < 2 else since, start=True, stop=True)
                    last.then_inc(side_ready, 1)
                token_major(N_VB, 2, None)
                token_major(N_VB, 3, None)
                for c in range(CH):
                    pe.wait_ge(cum_exp_done, L * 12 + 3 * (c + 1))
                    pe.matmul(side(f"tail{c}")[:, 0:256], after, la[c][:, 0:256], start=True, stop=True)
                    pe.matmul(side(f"tail{c}")[:, 256:512], before, la[c][:, 256:512],
                              start=True, stop=True).then_inc(side_ready, 1)
                for i in range(2):
                    pe.wait_ge(tail_done, L * 4 + (i + 1))
                    for c in (2 * i, 2 * i + 1):
                        for t in range(2):
                            last = pe.transpose(side(f"keys{i}")[:, (c % 2) * 256 + t * P:(c % 2) * 256 + (t + 1) * P],
                                                kT[t][:, c * P:(c + 1) * P], ident)
                    last.then_inc(side_ready, 1)
                token_major(N_VA, 0, lambda t: (vb_done, L * 4 + (t + 1)))
                token_major(N_VA, 1, None)
                for s in range(3):
                    if s < 2:
                        pe.wait_ge(tail_done, L * 4 + (s + 3))
                    pe.wait_ge(kend_done, L * 4 + 4)
                    for d, c in ((0, s), (1, CH - 1 - s)):
                        for h in range(HEADS):
                            a = (h % 2) * DK
                            last = pe.matmul(side(f"state{s}")[a:a + DK, (2 * d + h // 2) * P:(2 * d + h // 2 + 1) * P],
                                             kend[c][:, d * 256 + h * DK:d * 256 + (h + 1) * DK],
                                             vb[c][:, h * P:(h + 1) * P], start=True, stop=True)
                    last.then_inc(side_ready, 1)
                token_major(N_VA, 2, None)
                token_major(N_VA, 3, None)

                def scores(h):
                    a, pair = (h % 2) * DK, h // 2
                    for d, name in ((0, f"score_f{h}"), (1, f"score_b{h}")):
                        pe.wait_ge(*score_bank[name])
                        for c in range(CH):
                            w = slice(c * P, (c + 1) * P)
                            last = pe.matmul(side(name)[:, w], ki[2 * d + pair][a:a + DK, w],
                                             qd[2 * d + pair][a:a + DK, w], start=True, stop=True)
                        last.then_inc(side_ready, 1)

                score_bank = {
                    "score_f0": (kend_done, L * 4 + 4), "score_b0": (state_done, L * 9 + 1),
                    "score_f1": (state_done, L * 9 + 5), "score_b1": (state_done, L * 9 + 9),
                    "score_f2": (score_copied, L * 4 + 1), "score_b2": (score_done, L * 4 + 1),
                    "score_f3": (score_copied, L * 4 + 2), "score_b3": (score_done, L * 4 + 2)}

                def o_head(h):
                    a, pair = (h % 2) * DK, h // 2
                    pe.wait_ge(*((score_copied, L * 4 + 3), (score_done, L * 4 + 3),
                                 (score_copied, L * 4 + 4), (score_done, L * 4 + 4))[h])
                    pe.wait_ge(score_done, L * 4 + (h + 1))
                    for c in range(CH):
                        w = slice(c * P, (c + 1) * P)
                        out = side(f"o{h}")[:, w]
                        last = pe.matmul(out, vb[c][:, h * P:(h + 1) * P], A[h][:, w], start=True, stop=False)
                        if c > 0:
                            last = pe.matmul(out, state[a:a + DK, c - 1, 0, pair, :], qd[pair][a:a + DK, w],
                                             start=False, stop=(c == CH - 1))
                        if c < CH - 1:
                            last = pe.matmul(out, state[a:a + DK, 2 - c, 1, pair, :], qd[2 + pair][a:a + DK, w],
                                             start=False, stop=True)
                    last.then_inc(side_ready, 1)

                def mix(h):
                    for c in range(CH):
                        last = pe.matmul(side(f"mix{h}")[:, c * P:(c + 1) * P], va[:, (c * 4 + h) * P:(c * 4 + h + 1) * P],
                                         spatial_sb[:, h * P:(h + 1) * P], start=True, stop=True)
                    last.then_inc(side_ready, 1)

                for h in range(HEADS):
                    slab_wait(N_U + h)
                    pe.wait_ge(va_gelu, L * 4 + (h + 1))
                    project(h, xg)
                    if h == 0:
                        pe.wait_ge(qk_done, L * 8 + 8)
                        scores(0)
                    elif h == 1:
                        scores(1)
                        scores(2)
                    elif h == 2:
                        scores(3)
                        o_head(0)
                    else:
                        o_head(1)
                        o_head(2)
                        o_head(3)
                for h in range(HEADS):
                    slab_wait(N_G + h)
                    pe.wait_ge(u_lin, L * 4 + (h + 1))
                    project(h, xg)
                    if h == 0:
                        pe.wait_ge(vn_done, L * 8 + 8)
                        pe.wait_ge(og_done, L * 4 + 1)
                        mix(0)
                        pe.wait_ge(og_done, L * 4 + 2)
                        mix(1)
                    elif h == 1:
                        pe.wait_ge(osq_done, L * 4 + 4)
                        pe.wait_ge(og_done, L * 4 + 3)
                        for i in range(16):
                            last = pe.matmul(side("osum")[:, i:i + 1], osq[i // 4][:, (i % 4) * P:(i % 4 + 1) * P],
                                             ones[:, 0:1], start=True, stop=True)
                        last.then_inc(side_ready, 1)
                        pe.wait_ge(og_done, L * 4 + 4)
                        mix(2)
                        pe.wait_ge(mixed, L * 4 + 1)
                        mix(3)
                    else:
                        for i in (0, 1) if h == 2 else (2, 3):
                            pe.wait_ge(odiag_done, L * 4 + (i + 1))
                            pe.wait_ge(*((mixed, L * 4 + 2), (o_std_done, L + 1),
                                         (mixed, L * 4 + 3), (mixed, L * 4 + 4))[i])
                            spread(f"ospread{i}", odiag[i])
                with pe.Fori(0, KT // RING) as q:
                    for j in (1, 2, 3):
                        pe.wait_ge(lo_done, L * NS + q * RING + (N_OUT + j + 1 + RING))
                        pe.wait_ge(g_lin, L * 4 + (j + 1))
                        pe.wait_ge(x_done, L * NX + q * (j + 1) + RING)
                        if j == 1:
                            project_pair(feat, KT, (feat_ready, L * NF))
                        else:
                            project(j, feat)
                def up_first(slab, x_before, with_scale):
                    for j in range(RING):
                        slab_wait(slab + j)
                        pe.wait_ge(x_done, L * NX + (x_before + RING + j + 1 + RING))
                        project(j, xg, ready=(xg_ready, L * 16 + KT) if with_scale and j == 0 else None)
                        if with_scale and j == 0:
                            pe.wait_ge(o_normed, L * 4 + 1)
                            token_sums("ffn_sum", L * 2 + 1)
                        if with_scale and j == 1:
                            pe.wait_ge(diag_done, L * 2 + 2)
                            pe.wait_ge(o_normed, L * 4 + 2)
                            spread("ffn_spread", diag)

                def up_rest(slab, y_before, quads):
                    with pe.Fori(1, quads) as q:
                        for j in range(RING):
                            pe.wait_ge(lo_done, L * NS + q * RING + (slab + j + 1 + RING))
                            pe.wait_ge(y_ready, L * NY + q * RING + (y_before + j + 1 - RING))
                            project(j, xg)

                def down(slab, x_before, y_before, blocks, feats):
                    with pe.Fori(0, KT // RING) as q:
                        for j in (1, 2, 3):
                            pe.wait_ge(lo_done, L * NS + q * RING + (slab + j + 1 + RING))
                            pe.wait_ge(y_ready, L * NY + (y_before + j + 1))
                            pe.wait_ge(x_done, L * NX + q * (j + 1) + (x_before + RING))
                            if j == 1:
                                project_pair(feat, blocks, (feat_ready, L * NF + feats))
                            else:
                                project(j, feat, blocks)

                for part in range(FULL_PARTS + 1):
                    tiles = KT if part < FULL_PARTS else LAST_TILES
                    slab = N_FFN + part * PART
                    up_first(slab, part * KT, part == 0)
                    up_rest(slab, part * 2 * KT, tiles // 2)
                    down(slab + 2 * tiles, (part + 1) * KT, part * 2 * KT + 2 * tiles - RING, tiles,
                         (part + 1) * KT)

            token_sums("sum", 2 * DEPTH)
            pe.wait_ge(diag_done, 2 * DEPTH + 1)
            spread("spread", diag)


def kernel(x, g_mix, w_in, w_s, b_s, ln_g, ln_b, w_gate_f, b_gate_f, w_gate_b, b_gate_b,
           g_gla, w_out, g_ffn, w_up, conv_w, conv_b, w_down, g_final):
    import numpy as np
    import concourse.bacc as bacc
    from concourse.bass_utils import run_bass_kernel_spmd

    ins = [np.asarray(a) for a in (x, g_mix, w_in, w_s, b_s, ln_g, ln_b, w_gate_f, b_gate_f, w_gate_b, b_gate_b,
                                   g_gla, w_out, g_ffn, w_up, conv_w, conv_b, w_down, g_final)]
    (x, g_mix, w_in, w_s, b_s, ln_g, ln_b, w_gate_f, b_gate_f, w_gate_b, b_gate_b,
     g_gla, w_out, g_ffn, w_up, conv_w, conv_b, w_down, g_final) = ins
    f32 = np.float32

    def channel_major(w, rows, col):
        t = len(rows) // P
        out = np.zeros((P, SLAB), f32)
        out[:, :t * P] = w[rows.start:rows.stop, col:col + P].reshape(t, P, P).transpose(1, 0, 2).reshape(P, t * P)
        return out

    def token_major(w, s, col):
        return w[2 * s * P:2 * (s + 1) * P, col:col + S].reshape(2, P, S).transpose(1, 0, 2).reshape(P, SLAB)

    A_W = B_W = 512
    QK = HEADS * DK
    U, VA, Q, K, VB, G = 0, A_W, 2 * A_W, 2 * A_W + QK, 2 * A_W + 2 * QK, 2 * A_W + 2 * QK + B_W
    R = G + B_W
    every = range(0, D)
    slabs = []
    for l in range(DEPTH):
        slabs += [channel_major(w_in[l], every, c) for c in (K, K + P, Q, Q + P)]
        slabs += [token_major(w_in[l], s, VB) for s in range(4)]
        slabs += [token_major(w_in[l], s, VA) for s in range(4)]
        slabs += [channel_major(w_in[l], every, U + h * P) for h in range(4)]
        slabs += [channel_major(w_in[l], every, G + h * P) for h in range(4)]
        slabs += [channel_major(w_out[l], every, m * P) for m in range(KT)]
        for first in range(0, FT, KT):
            tiles = range(first, min(first + KT, FT))
            for f in tiles:
                slabs += [channel_major(w_up[l], every, f * P), channel_major(w_up[l], every, DFF + f * P)]
            rows = range(tiles.start * P, tiles.stop * P)
            slabs += [channel_major(w_down[l], rows, m * P) for m in range(KT)]
    slabs = np.stack(slabs)
    gate = np.zeros((DEPTH, 2 * RANK + 1, 2 * QK), f32)
    gate[:, :RANK, :QK] = w_gate_f
    gate[:, RANK:2 * RANK, QK:] = w_gate_b
    gate[:, 2 * RANK, :QK] = b_gate_f
    gate[:, 2 * RANK, QK:] = b_gate_b
    gains = np.stack([g_mix[0], g_ffn[0], g_mix[1], g_ffn[1], g_final])
    j, i = np.arange(P)[:, None], np.arange(P)[None, :]
    arrays = {
        "xT": x[0].T,
        "slabs": slabs,
        "rank_w": w_in[:, :, R:].reshape(DEPTH, KT, P, 2 * RANK).transpose(2, 0, 1, 3).reshape(P, -1),
        "gate_w": gate,
        "spatial_w": w_s.transpose(0, 3, 1, 2).reshape(DEPTH, P, HEADS * P),
        "spatial_b": b_s.reshape(DEPTH, HEADS * P),
        "ln_gb": np.concatenate([ln_g.reshape(DEPTH, -1), ln_b.reshape(DEPTH, -1)], 1),
        "gains": gains.reshape(2 * DEPTH + 1, KT, P).transpose(2, 0, 1).reshape(P, -1),
        "gla_gain": g_gla.reshape(DEPTH * HEADS, P).T,
        "conv": np.concatenate([conv_w, conv_b[:, None]], 1).reshape(DEPTH, 4, 2, FT, P)
                  .transpose(4, 0, 3, 2, 1).reshape(P, -1),
        "consts": np.concatenate([j == i, j <= i, j >= i, j > i, j < i], 1).astype(f32),
    }
    arrays = {n: np.ascontiguousarray(a) for n, a in arrays.items()}
    nc = bacc.Bacc("TRN2", target_bir_lowering=False, num_devices=1)
    args = [nc.dram_tensor(n, a.shape, F32, kind="ExternalInput").ap() for n, a in arrays.items()]
    args.append(nc.dram_tensor("outT", (D, S), F32, kind="ExternalOutput").ap())
    encoder(nc, *args)
    r = run_bass_kernel_spmd(nc, [arrays], core_ids=[0])
    return np.ascontiguousarray(r.results[0]["outT"].T)[None]
```

```python
from contextlib import ExitStack

import concourse.bass as bass
from concourse import mybir

F32 = mybir.dt.float32
F32R = mybir.dt.float32r
U32 = mybir.dt.uint32
ALU = mybir.AluOpType
ACT = mybir.ActivationFunctionType

P = 128
D, S, DEPTH = 1024, 512, 2
KT = D // P
CH = S // P
HEADS, DK = 4, 64
RANK = 16
DFF = 2816
FT = DFF // P
FULL_PARTS = 2
LAST_TILES = FT - FULL_PARTS * KT
EPS = 1e-6

RING = 4
SLAB = KT * P
N_K, N_Q, N_VB, N_VA, N_U, N_G, N_OUT = 0, 2, 4, 8, 12, 16, 20
N_FFN = N_OUT + KT
PART = 3 * KT
N_LAST = N_FFN + FULL_PARTS * PART
NS = N_LAST + 2 * LAST_TILES + KT
assert NS % RING == 0 and N_FFN % RING == 0 and N_LAST % RING == 0 and LAST_TILES % 2 == 0

SIDE = (["rankT", "spread", "sum"] + [f"z{t}" for t in range(4)] + [f"cum{t}" for t in range(4)]
        + [f"keys{c}" for c in range(4)] + [f"state{s}" for s in range(3)]
        + [f"score_{d}{h}" for h in range(4) for d in "fb"] + [f"o{h}" for h in range(4)]
        + ["mix0", "mix1", "osum", "mix2", "mix3"] + [f"ospread{h}" for h in range(4)]
        + ["ffn_spread"])
NSIDE = len(SIDE)


def encoder(nc, xT, slabs, rank_w, gate_w, spatial_w, spatial_b, ln_gb, gains, gla_gain, conv, consts, outT):
    with ExitStack() as ctx:
        def sb(name, shape, dt=F32):
            return ctx.enter_context(nc.sbuf_tensor(name, shape, dt))

        def sem(name):
            return ctx.enter_context(nc.semaphore(name))

        x = sb("x", [P, KT * S])
        xg_hi = sb("xg_hi", [P, KT * S], F32R)
        xg_lo = sb("xg_lo", [P, KT * S], F32R)
        feat_hi = sb("feat_hi", [P, 4 * S], F32R)
        feat_lo = sb("feat_lo", [P, 4 * S], F32R)
        with nc.sbuf_tensor("u", [P, 4 * S], F32) as u:
            pass
        feat2_hi = sb("feat2_hi", [P, 4 * S], F32R)
        with nc.sbuf_tensor("va", [P, 4 * S], F32) as va:
            pass
        feat2_lo = sb("feat2_lo", [P, 4 * S], F32R)
        w_raw = sb("w_raw", [P, RING * SLAB])
        w_hi = sb("w_hi", [P, RING * SLAB], F32R)
        w_lo = sb("w_lo", [P, RING * SLAB], F32R)
        arena = sb("arena", [P, 23 * S])
        rstdT = sb("rstdT", [P, S])
        ssq = sb("ssq", [P, S])
        rankT = sb("rankT", [4 * RANK + 1, S])
        rank_raw = sb("rank_raw", [P, (DEPTH + 1) * KT * 2 * RANK])
        RW = KT * 2 * RANK
        rank_split = sb("rank_split", [P, 2 * RW + P - 4 * RANK], F32R)
        gate_sb = sb("gate_sb", [4 * RANK + 1, 4 * P])
        spatial_sb = sb("spatial_sb", [P, HEADS * P])
        spatial_b_sb = sb("spatial_b_sb", [P, HEADS * P])
        ln_sb = sb("ln_sb", [P, 2 * HEADS * P])
        gains_sb = sb("gains_sb", [P, (2 * DEPTH + 1) * KT])
        gla_sb = sb("gla_sb", [P, DEPTH * HEADS])
        conv_sb = sb("conv_sb", [P, DEPTH * FT * 8])
        consts_sb = sb("consts_sb", [P, 4 * P])
        ones_r = sb("ones_r", [P, P], F32R)
        ones = ones_r[:, :].bitcast(F32)
        eps = sb("eps", [P, 1])
        std = sb("std", [P, CH])
        rstd = sb("rstd", [P, CH])
        total = sb("total", [P, 4 * CH])
        decay = sb("decay", [P, 4 * CH])
        bn = sb("bn", [P, 16 * 6])
        mv = sb("mv", [P, 16 * 2])
        ln_std = sb("ln_std", [P, 16])
        ln_rstd = sb("ln_rstd", [P, 16])
        o_std = sb("o_std", [P, 16])
        o_rstd = sb("o_rstd", [P, 16])
        o_rstd_parts = sb("o_rstd_parts", [P, 2 * 16], F32R)

        ident, upto, since, after = (consts_sb[:, i * P:(i + 1) * P] for i in range(4))

        def slot(i, n=1):
            return arena[:, i * S:(i + n) * S]

        kT, qT = [slot(0), slot(1)], [slot(2), slot(3)]
        A = [slot(h) for h in range(4)]
        la = [slot(4 + t) for t in range(4)]
        keT = la
        kend = [slot(c) for c in range(4)]
        osq = la
        softplus = [slot(12 + t) for t in range(4)]
        qd = [slot(8 + t) for t in range(4)]
        diag = slot(11)
        odiag = [[part[:, h * S:(h + 1) * S] for h in range(4)] for part in (feat2_hi, feat2_lo)]
        ki = [slot(12 + t) for t in range(4)]
        g = ki
        sq = [slot(12 + i) for i in range(8)]
        vb = [slot(16 + t) for t in range(4)]
        mt = vb
        state = arena[:, 20 * S:23 * S].rearrange("p (s d r e) -> p s d r e", s=3, d=2, r=2)
        YW = S + 2
        y = [arena[:, i * YW:(i + 1) * YW] for i in range(4)]
        z = [arena[:, 4 * YW + i * S:4 * YW + (i + 1) * S] for i in range(4)]
        gated = [arena[:, 4 * YW + (4 + i) * S:4 * YW + (5 + i) * S] for i in range(2)]

        acc = [ctx.enter_context(nc.psum_tensor(f"acc{i}", [P, S], F32)) for i in range(RING)]
        side_banks = [ctx.enter_context(nc.psum_tensor(f"side{i}", [P, S], F32)) for i in range(RING)]
        side_at = {name: i for i, name in enumerate(SIDE)}

        def side(name):
            return side_banks[side_at[name] % RING]

        def featT(hi, k):
            if k < 4:
                return (feat_hi if hi else feat_lo)[:, k * S:(k + 1) * S]
            return (feat2_hi if hi else feat2_lo)[:, (k - 4) * S:(k - 3) * S]

        def rank_part(lo):
            return rank_split[:, 0:2 * RW].rearrange("p (k two r) -> p k two r", k=KT, two=2)[:, :, lo, :]

        def rank_of(L):
            return rank_raw[:, bass.ds(L * RW, RW)].rearrange("p (k r) -> p k r", k=KT)

        def xg_out(m):
            return slot(12 + m)

        x_loaded = [sem(f"x_loaded{i}") for i in range(4)]
        gains_loaded, par_loaded = sem("gains_loaded"), sem("par_loaded")
        rank_loaded, vec_loaded = sem("rank_loaded"), sem("vec_loaded")
        raw_loaded = [sem(f"raw_loaded{i}") for i in range(RING)]
        hi_done, lo_done = sem("hi_done"), sem("lo_done")
        group_used = sem("group_used")
        acc_ready = sem("acc_ready")
        side_ready = sem("side_ready")
        ones_set, setup_done = sem("ones_set"), sem("setup_done")
        rank_hi_done, rank_lo_done = sem("rank_hi_done"), sem("rank_lo_done")
        xg_hi_done, xg_ready = sem("xg_hi_done"), sem("xg_ready")
        sq_done, ssq_added = sem("sq_done"), sem("ssq_added")
        std_done, rstd_done = sem("std_done"), sem("rstd_done")
        stdT_done, rstdT_done = sem("stdT_done"), sem("rstdT_done")
        diag_done = sem("diag_done")
        kT_done, qT_done = sem("kT_done"), sem("qT_done")
        rankT_done = sem("rankT_done")
        softplus_done, la_done = sem("softplus_done"), sem("la_done")
        total_done = sem("total_done")
        cum_exp_done = sem("cum_exp_done")
        end_exp_done = sem("end_exp_done")
        qk_done = sem("qk_done")
        vb_done = sem("vb_done")
        keT_done, kend_done = sem("keT_done"), sem("kend_done")
        state_done = sem("state_done")
        va_gelu = sem("va_gelu")
        bn_done, mv_done = sem("bn_done"), sem("mv_done")
        ln_std_done, ln_rstd_done = sem("ln_std_done"), sem("ln_rstd_done")
        vhat_done, vn_done = sem("vhat_done"), sem("vn_done")
        u_lin, u_gelu = sem("u_lin"), sem("u_gelu")
        score_copied, score_done = sem("score_copied"), sem("score_done")
        osq_done, og_done = sem("osq_done"), sem("og_done")
        g_lin, g_silu = sem("g_lin"), sem("g_silu")
        mixed, u_mixed = sem("mixed"), sem("u_mixed")
        o_std_done, o_rstd_done, odiag_done = sem("o_std_done"), sem("o_rstd_done"), sem("odiag_done")
        o_normed, o_gated = sem("o_normed"), sem("o_gated")
        feat_hi_done, feat_ready = sem("feat_hi_done"), sem("feat_ready")
        x_done = sem("x_done")
        halo = sem("halo")
        y_ready, centre_done, taps_done = sem("y_ready"), sem("centre_done"), sem("taps_done")
        silu_done, gated_done = sem("silu_done"), sem("gated_done")
        final_done, out_stored = sem("final_done"), sem("out_stored")
        waits_passed = sem("waits_passed")
        NF = KT + FT
        NX = 4 * KT
        NY = 2 * FT

        def on_its_own(eng):
            eng.sem_inc(waits_passed, 1)

        block = ctx.enter_context(nc.Block())

        @block.sync
        def _(sp):
            def load_slab(L, q, j):
                sp.wait_ge(lo_done, L * NS + q * RING + (j + 1))
                sp.dma_start(w_raw[:, j * SLAB:(j + 1) * SLAB],
                             slabs[bass.ds(L * NS + q * RING + j, 1), :, :].rearrange("o p n -> (o p) n")
                             ).then_inc(raw_loaded[j], 16)

            with sp.Fori(0, DEPTH) as L:
                for j in range(RING):
                    load_slab(L, 0, j)
                with sp.If(L < 1):
                    sp.dma_start(rank_raw[:, 0:DEPTH * RW], rank_w).then_inc(rank_loaded, 16)
                    sp.dma_start(consts_sb[:, :], consts).then_inc(vec_loaded, 16)
                    sp.dma_start(gla_sb[:, :], gla_gain).then_inc(vec_loaded, 16)
                    sp.dma_start(conv_sb[:, :], conv).then_inc(vec_loaded, 16)
                for dst, src in (
                        (gate_sb[:, :], gate_w[bass.ds(L, 1), :, :].rearrange("o p n -> (o p) n")),
                        (spatial_sb[:, :], spatial_w[bass.ds(L, 1), :, :].rearrange("o p n -> (o p) n")),
                        (spatial_b_sb[:, :], spatial_b[bass.ds(L, 1), :].broadcast_to([P, HEADS * P])),
                        (ln_sb[:, :], ln_gb[bass.ds(L, 1), :].broadcast_to([P, 2 * HEADS * P]))):
                    sp.dma_start(dst, src).then_inc(par_loaded, 16)
                with sp.Fori(1, NS // RING) as q:
                    for j in range(RING):
                        load_slab(L, q, j)
            for m in range(KT):
                sp.wait_ge(final_done, m + 1)
                sp.dma_start(outT[m * P:(m + 1) * P, :], xg_out(m)).then_inc(out_stored, 16)
            sp.wait_ge(out_stored, 16 * KT)

        @block.gpsimd
        def _(pool):
            pool.memset(ones, 1.0).then_inc(ones_set, 1)
            pool.memset(rank_split[:, 2 * RW:2 * RW + P - 4 * RANK].bitcast(F32), 0.0).then_inc(setup_done, 1)
            pool.memset(eps[:, :], EPS).then_inc(lo_done, RING)
            with pool.Fori(0, DEPTH * NS // RING) as q:
                for j in range(RING):
                    w = slice(j * SLAB, (j + 1) * SLAB)
                    pool.wait_ge(hi_done, q * RING + (j + 1))
                    pool.tensor_tensor(w_lo[:, w], w_raw[:, w], w_hi[:, w].bitcast(F32),
                                       ALU.subtract).then_inc(lo_done, 1)

        @block.scalar
        def _(act):
            def split_hi(j):
                w = slice(j * SLAB, (j + 1) * SLAB)
                act.activation(w_hi[:, w], w_raw[:, w], ACT.Copy).then_inc(hi_done, 1)

            def split_after(L, n):
                act.wait_ge(raw_loaded[n % RING], 16 * (L * (NS // RING)) + 16 * (n // RING + 2))
                split_hi(n % RING)

            def gain_hi(m, r):
                act.activation(xg_hi[:, bass.ds(m * S, S)], x[:, bass.ds(m * S, S)], ACT.Copy,
                               scale=gains_sb[:, bass.ds(r * KT + m, 1)]).then_inc(xg_hi_done, 1)

            def square(m, r, buffer):
                act.activation(sq[buffer], x[:, bass.ds(m * S, S)], ACT.Square).then_inc(sq_done, 1)

            def emit(m, j, r, x_count, final_norm_after):
                act.wait_ge(*x_count)
                on_its_own(act)
                if not final_norm_after:
                    gain_hi(m, r)
                act.wait_ge(ssq_added, r * (KT + 1) + m)
                on_its_own(act)
                square(m, r, j % 2)
                if final_norm_after:
                    with act.If(r < 2 * DEPTH):
                        gain_hi(m, r)

            def root(name, done, count, r_ap, scale, n):
                act.wait_ge(side_ready, count)
                act.activation(r_ap, side(name)[:, 0:n], ACT.Sqrt, bias=eps[:, 0:1], scale=scale).then_inc(done, 1)

            act.dma_start(gains_sb[:, :], gains).then_inc(gains_loaded, 16)
            for c in range(4):
                rows = xT[c * 2 * P:(c + 1) * 2 * P, :].rearrange("(k p) s -> p k s", p=P)
                act.dma_start(x[:, c * 2 * S:(c + 1) * 2 * S].rearrange("p (k s) -> p k s", k=2),
                              rows).then_inc(x_loaded[c], 16)
            act.wait_ge(ones_set, 1)
            act.activation(std[:, 0:1], ones[:, 0:1], ACT.Copy)

            def rank_hi(L):
                act.activation(rank_part(0), rank_of(L), ACT.Copy).then_inc(rank_hi_done, 1)

            act.wait_ge(gains_loaded, 16)

            def load_and_split(c):
                act.wait_ge(x_loaded[c], 16)
                gain_hi(2 * c, 0)
                gain_hi(2 * c + 1, 0)
                act.wait_ge(raw_loaded[c], 16)
                split_hi(c)

            load_and_split(0)
            load_and_split(1)
            square(0, 0, 0)
            square(1, 0, 1)
            load_and_split(2)
            load_and_split(3)
            act.wait_ge(rank_loaded, 16)
            rank_hi(0)
            for m in range(2, KT):
                square(m, 0, m)

            with act.Fori(0, DEPTH) as L:
                def acc_at(n):
                    act.wait_ge(acc_ready, L * NS + n)

                def side_wait(name):
                    act.wait_ge(side_ready, L * NSIDE + (side_at[name] + 1))

                acc_at(1)
                split_after(L, 0)
                acc_at(2)
                split_after(L, 1)
                root("spread", stdT_done, L * NSIDE + 2, rstdT[:, :], 1.0 / D, S)
                root("sum", std_done, L * NSIDE + 3, std[:, :], 1.0 / D, CH)
                with act.If(L < DEPTH - 1):
                    rank_hi(L + 1)
                acc_at(3)
                split_after(L, 2)
                for t in range(CH):
                    side_wait(f"z{t}")
                    act.activation(softplus[t], side(f"z{t}")[:, :], ACT.Abs).then_inc(softplus_done, 1)
                    act.wait_ge(softplus_done, L * 12 + (2 * t + 1))
                    act.activation(softplus[t], softplus[t], ACT.Exp, scale=-1.0).then_inc(softplus_done, 1)
                acc_at(4)
                split_after(L, 3)
                for t in range(CH):
                    act.wait_ge(softplus_done, L * 12 + (2 * t + 2))
                    act.activation(softplus[t], softplus[t], ACT.Ln, bias=ones[:, 0:1]).then_inc(softplus_done, 1)
                act.wait_ge(group_used, L * 6 + 1)
                split_after(L, 4)
                act.wait_ge(group_used, L * 6 + 2)
                split_after(L, 5)
                for t in range(4):
                    side_wait(f"cum{t}")
                    cum = side(f"cum{t}")
                    act.wait_ge(la_done, L * 4 + 4)
                    act.activation(qd[t], cum[:, :], ACT.Exp, scale=1.0 / 16).then_inc(cum_exp_done, 1)
                    act.activation(ki[t], cum[:, :], ACT.Exp, scale=-1.0 / 16).then_inc(cum_exp_done, 1)
                    edge = P - 1 if t < 2 else 0
                    act.activation(decay[:, t * CH:(t + 1) * CH],
                                   cum[:, :].rearrange("p (c i) -> p c i", c=CH)[:, :, edge],
                                   ACT.Exp, scale=1.0 / 16).then_inc(cum_exp_done, 1)
                    act.activation(total[:, t * CH:(t + 1) * CH],
                                   cum[:, :].rearrange("p (c i) -> p c i", c=CH)[:, :, edge],
                                   ACT.Copy, scale=1.0 / 16).then_inc(total_done, 1)
                for t in range(4):
                    act.wait_ge(total_done, L * 4 + (t + 1))
                    for c in range(CH):
                        w = slice(c * P, (c + 1) * P)
                        act.activation(keT[t][:, w], side(f"cum{t}")[:, w], ACT.Exp, scale=-1.0 / 16,
                                       bias=total[:, t * CH + c:t * CH + c + 1]).then_inc(end_exp_done, 1)
                act.wait_ge(group_used, L * 6 + 3)
                split_after(L, 6)
                for t in range(CH):
                    acc_at(N_VB + t + 1)
                    if t == CH - 1:
                        split_after(L, 7)
                    act.activation(vb[t], acc[t][:, :], ACT.Copy, scale=rstd[:, t:t + 1]).then_inc(vb_done, 1)
                act.wait_ge(group_used, L * 6 + 4)
                split_after(L, 8)
                act.wait_ge(group_used, L * 6 + 5)
                split_after(L, 9)
                act.wait_ge(group_used, L * 6 + 6)
                split_after(L, 10)
                for t in range(CH):
                    acc_at(N_VA + t + 1)
                    if t == CH - 1:
                        split_after(L, 11)
                    act.activation(va[:, t * S:(t + 1) * S], acc[t][:, :], ACT.Gelu,
                                   scale=rstd[:, t:t + 1]).then_inc(va_gelu, 1)

                def copy_score(h):
                    side_wait(f"score_f{h}")
                    act.activation(A[h], side(f"score_f{h}")[:, :], ACT.Copy).then_inc(score_copied, 1)

                def gelu_u(h):
                    act.wait_ge(u_lin, L * 4 + (h + 1))
                    uh = u[:, h * S:(h + 1) * S]
                    act.activation(uh, uh, ACT.Gelu).then_inc(u_gelu, 1)

                def square_o(h):
                    side_wait(f"o{h}")
                    act.activation(osq[h], side(f"o{h}")[:, :], ACT.Square).then_inc(osq_done, 1)

                acc_at(N_U + 1)
                split_after(L, 12)
                copy_score(0)
                act.wait_ge(mv_done, L * 16 + 16)
                act.activation(ln_std[:, :], mv[:, :].rearrange("p (a b) -> p a b", b=2)[:, :, 1], ACT.Sqrt,
                               bias=eps[:, 0:1]).then_inc(ln_std_done, 1)
                gelu_u(0)
                acc_at(N_U + 2)
                split_after(L, 13)
                copy_score(1)
                copy_score(2)
                gelu_u(1)
                acc_at(N_U + 3)
                split_after(L, 14)
                copy_score(3)
                gelu_u(2)
                square_o(0)
                acc_at(N_U + 4)
                split_after(L, 15)
                gelu_u(3)
                square_o(1)
                square_o(2)
                square_o(3)

                def hi_of(count, src, k):
                    act.wait_ge(*count)
                    act.activation(featT(True, k), src, ACT.Copy).then_inc(feat_hi_done, 1)

                def silu_g(h):
                    act.wait_ge(g_lin, L * 4 + (h + 1))
                    act.activation(g[h], g[h], ACT.Silu).then_inc(g_silu, 1)

                acc_at(N_G + 1)
                split_after(L, 16)
                hi_of((u_mixed, L * 4 + 1), mt[0], 0)
                hi_of((u_mixed, L * 4 + 2), mt[1], 1)
                root("osum", o_std_done, L * NSIDE + (side_at["osum"] + 1), o_std[:, :], 1.0 / P, 16)
                acc_at(N_G + 2)
                split_after(L, 17)
                hi_of((u_mixed, L * 4 + 3), mt[2], 2)
                hi_of((u_mixed, L * 4 + 4), mt[3], 3)
                acc_at(N_G + 3)
                split_after(L, 18)
                silu_g(0)
                silu_g(1)
                hi_of((o_gated, L * 4 + 1), mt[0], 4)
                silu_g(2)
                acc_at(N_G + 4)
                split_after(L, 19)
                hi_of((o_gated, L * 4 + 2), mt[1], 5)
                silu_g(3)
                hi_of((o_gated, L * 4 + 3), mt[2], 6)
                hi_of((o_gated, L * 4 + 4), mt[3], 7)

                with act.Fori(0, KT // RING) as q:
                    for j in range(RING):
                        m = q * RING + j
                        act.wait_ge(acc_ready, L * NS + q * RING + (N_OUT + j + 1))
                        act.wait_ge(raw_loaded[j], 16 * (L * (NS // RING)) + 16 * q + 16 * (N_OUT // RING + 2))
                        split_hi(j)
                        emit(m, j, L * 2 + 1, (x_done, L * NX + m + (1 + RING)), False)

                root("ffn_spread", stdT_done, L * NSIDE + NSIDE, rstdT[:, :], 1.0 / D, S)

                def up_quad(slab, tile, feat):
                    for b in range(2):
                        f = L * FT + tile + b
                        for v in range(2):
                            j = 2 * b + v
                            coef = (f * 2 + v) * 4
                            act.wait_ge(y_ready, f * 2 + v + 1)
                            on_its_own(act)
                            act.activation(z[j], y[j][:, 1:S + 1], ACT.Identity,
                                           scale=conv_sb[:, bass.ds(coef + 1, 1)],
                                           bias=conv_sb[:, bass.ds(coef + 3, 1)]).then_inc(centre_done, 1)
                            act.wait_ge(raw_loaded[j], 16 * (L * (NS // RING)) + 4 * slab + 32)
                            split_hi(j)
                            if v == 0:
                                act.wait_ge(taps_done, f * 4 + 2)
                                act.activation(z[j], z[j], ACT.Silu).then_inc(silu_done, 1)
                        act.wait_ge(gated_done, f + 1)
                        on_its_own(act)
                        act.activation(feat(b), gated[b], ACT.Copy).then_inc(feat_hi_done, 1)

                def down(slab, last):
                    with act.Fori(0, KT // RING) as q:
                        for j in range(RING):
                            m = q * RING + j
                            act.wait_ge(acc_ready, L * NS + slab + q * RING + (j + 1))
                            if not last:
                                act.wait_ge(raw_loaded[j], 16 * (L * (NS // RING)) + 4 * slab + 16 * q + 32)
                                split_hi(j)
                            else:
                                with act.If(L * NS + q * RING + (slab + j + RING) < DEPTH * NS):
                                    act.wait_ge(raw_loaded[j], 16 * (L * (NS // RING)) + 4 * slab + 16 * q + 32)
                                    split_hi(j)
                                emit(m, j, L * 2 + 2, (x_done, L * NX + m + (NX - KT + 1 + RING)), True)

                with act.Fori(0, FULL_PARTS) as part:
                    for half, dst in ((0, feat_hi), (1, feat2_hi)):
                        with act.Fori(0, 2) as q:
                            up_quad(part * PART + q * RING + (N_FFN + half * 8), part * KT + q * 2 + half * 4,
                                    lambda b: dst[:, bass.ds(q * (2 * S) + b * S, S)])
                    down(part * PART + (N_FFN + 2 * KT), False)
                for q in range(LAST_TILES // 2):
                    up_quad(N_LAST + q * RING, FULL_PARTS * KT + 2 * q, lambda b: featT(True, 2 * q + b))
                act.activation(ln_std[:, 0:1], ones[:, 0:1], ACT.Sqrt)
                down(N_LAST + 2 * LAST_TILES, True)

            root("sum", std_done, DEPTH * NSIDE + 1, std[:, :], 1.0 / D, CH)

        @block.vector
        def _(dve):
            def gain_lo(m, r):
                w = bass.ds(m * S, S)
                dve.wait_ge(xg_hi_done, r * KT + m + 1)
                dve.scalar_tensor_tensor(out=xg_lo[:, w], in0=x[:, w], scalar=gains_sb[:, bass.ds(r * KT + m, 1)],
                                         in1=xg_hi[:, w].bitcast(F32), op0=ALU.mult,
                                         op1=ALU.subtract).then_inc(xg_ready, 1)

            def add_square(m, r, buffer):
                dve.wait_ge(sq_done, r * KT + m + 1)
                dve.wait_ge(ssq_added, r * (KT + 1) + m + 1)
                dve.tensor_tensor(ssq[:, :], ssq[:, :], sq[buffer], ALU.add).then_inc(ssq_added, 1)

            def token_scale(r):
                dve.wait_ge(stdT_done, r + 1)
                dve.reciprocal(rstdT[:, :], rstdT[:, :]).then_inc(rstdT_done, 1)

            def token_scale_on_partitions(L):
                dve.wait_ge(std_done, L + 1)
                dve.reciprocal(rstd[:, :], std[:, :]).then_inc(rstd_done, 1)

            def start_squares():
                dve.memset(ssq[:, :], 0.0).then_inc(ssq_added, 1)

            def rank_lo(L):
                dve.wait_ge(rank_hi_done, L + 1)
                dve.tensor_tensor(rank_part(1), rank_of(L), rank_part(0).bitcast(F32),
                                  ALU.subtract).then_inc(rank_lo_done, 1)

            dve.memset(ssq[:, :], 0.0).then_inc(ssq_added, 1)
            dve.memset(rankT[4 * RANK:4 * RANK + 1, :], 1.0).then_inc(setup_done, 1)
            dve.sem_inc(x_done, RING)
            dve.wait_ge(gains_loaded, 16)
            for m in range(0, 4):
                gain_lo(m, 0)
            add_square(0, 0, 0)
            add_square(1, 0, 1)
            for m in range(4, KT):
                gain_lo(m, 0)
            rank_lo(0)
            for m in range(2, KT):
                add_square(m, 0, m)
            dve.wait_ge(vec_loaded, 3 * 16)
            with dve.Fori(0, DEPTH) as L:
                def acc_at(n):
                    dve.wait_ge(acc_ready, L * NS + n)

                def side_wait(name):
                    dve.wait_ge(side_ready, L * NSIDE + (side_at[name] + 1))

                token_scale(L * 2)
                token_scale_on_partitions(L)
                start_squares()
                dve.wait_ge(rstdT_done, L * 2 + 1)
                side_wait("rankT")
                dve.tensor_tensor(rankT[0:4 * RANK, :], side("rankT")[0:4 * RANK, :], rstdT[0:4 * RANK, :],
                                  ALU.mult).then_inc(rankT_done, 1)
                with dve.If(L < DEPTH - 1):
                    rank_lo(L + 1)
                for t in range(2):
                    acc_at(N_K + t + 1)
                    dve.tensor_tensor(kT[t], acc[t][:, :], rstdT[:, :], ALU.mult).then_inc(kT_done, 1)
                for t in range(2):
                    acc_at(N_Q + t + 1)
                    dve.scalar_tensor_tensor(out=qT[t], in0=acc[2 + t][:, :], scalar=DK ** -0.5, in1=rstdT[:, :],
                                             op0=ALU.mult, op1=ALU.mult).then_inc(qT_done, 1)
                for t in range(CH):
                    dve.wait_ge(softplus_done, L * 12 + (8 + t + 1))
                    dve.scalar_tensor_tensor(out=la[t], in0=side(f"z{t}")[:, :], scalar=0.0, in1=softplus[t],
                                             op0=ALU.min, op1=ALU.subtract).then_inc(la_done, 1)
                dve.wait_ge(qT_done, L * 2 + 2)
                for t in range(4):
                    dve.wait_ge(cum_exp_done, L * 12 + (3 * t + 2))
                    dve.tensor_tensor(qd[t], qd[t], qT[t % 2], ALU.mult).then_inc(qk_done, 1)
                    dve.tensor_tensor(ki[t], ki[t], kT[t % 2], ALU.mult).then_inc(qk_done, 1)
                for t in range(4):
                    dve.wait_ge(end_exp_done, L * 16 + 4 * (t + 1))
                    dve.tensor_tensor(keT[t], keT[t], kT[t % 2], ALU.mult).then_inc(keT_done, 1)
                for c in range(CH):
                    side_wait(f"keys{c}")
                    dve.tensor_copy(kend[c], side(f"keys{c}")[:, :]).then_inc(kend_done, 1)
                side_wait("state0")
                dve.wait_ge(cum_exp_done, L * 12 + 12)
                dve.tensor_copy(state[:, 0, :, :, :].rearrange("p d r e -> p (d r e)"),
                                side("state0")[:, :]).then_inc(state_done, 1)
                for s in range(1, 3):
                    side_wait(f"state{s}")
                    dve.wait_ge(state_done, L * 9 + (1 + 4 * (s - 1)))
                    for dr in range(4):
                        chunk = s if dr < 2 else CH - 1 - s
                        dve.scalar_tensor_tensor(out=state[:, s, dr // 2, dr % 2, :],
                                                 in0=state[:, s - 1, dr // 2, dr % 2, :],
                                                 scalar=decay[:, dr * CH + chunk:dr * CH + chunk + 1],
                                                 in1=side(f"state{s}")[:, dr * P:(dr + 1) * P],
                                                 op0=ALU.mult, op1=ALU.add).then_inc(state_done, 1)
                for t in range(CH):
                    dve.wait_ge(va_gelu, L * 4 + (t + 1))
                    for h in range(HEADS):
                        i = t * HEADS + h
                        dve.bn_stats(bn[:, i * 6:(i + 1) * 6], va[:, i * P:(i + 1) * P]).then_inc(bn_done, 1)
                    for h in range(HEADS):
                        i = t * HEADS + h
                        dve.wait_ge(bn_done, L * 16 + (i + 1))
                        on_its_own(dve)
                        dve.bn_aggr(mv[:, i * 2:(i + 1) * 2], bn[:, i * 6:(i + 1) * 6]).then_inc(mv_done, 1)

                def scale_u(h):
                    acc_at(N_U + h + 1)
                    dve.tensor_tensor(u[:, h * S:(h + 1) * S], acc[h][:, :], rstdT[:, :], ALU.mult).then_inc(u_lin, 1)

                def select_scores(h):
                    side_wait(f"score_b{h}")
                    dve.wait_ge(score_copied, L * 4 + (h + 1))
                    on_its_own(dve)
                    dve.copy_predicated(A[h].rearrange("p (c i) -> p c i", c=CH),
                                        after.bitcast(U32).unsqueeze(1).broadcast_to([P, CH, P]),
                                        side(f"score_b{h}")[:, :].rearrange("p (c i) -> p c i", c=CH)
                                        ).then_inc(score_done, 1)

                def layernorm(t):
                    for h in range(HEADS):
                        i = t * HEADS + h
                        vi = va[:, i * P:(i + 1) * P]
                        dve.tensor_scalar(vi, vi, mv[:, i * 2:i * 2 + 1], ln_rstd[:, i:i + 1],
                                          ALU.subtract, ALU.mult).then_inc(vhat_done, 1)
                    vt = va[:, t * S:(t + 1) * S]
                    dve.wait_ge(vhat_done, L * 16 + 4 * (t + 1))
                    dve.tensor_tensor(vt, vt, ln_sb[:, 0:S], ALU.mult).then_inc(vn_done, 1)
                    dve.wait_ge(vn_done, L * 8 + (2 * t + 1))
                    dve.tensor_tensor(vt, vt, ln_sb[:, S:2 * S], ALU.add).then_inc(vn_done, 1)

                def gain_o(h):
                    dve.wait_ge(osq_done, L * 4 + (h + 1))
                    dve.tensor_scalar(A[h], side(f"o{h}")[:, :], gla_sb[:, bass.ds(L * HEADS + h, 1)], None,
                                      ALU.mult).then_inc(og_done, 1)

                scale_u(0)
                select_scores(0)
                dve.wait_ge(ln_std_done, L + 1)
                dve.reciprocal(ln_rstd[:, :], ln_std[:, :]).then_inc(ln_rstd_done, 1)
                dve.wait_ge(ln_rstd_done, L + 1)
                dve.wait_ge(par_loaded, L * 64 + 64)
                layernorm(0)
                scale_u(1)
                select_scores(1)
                select_scores(2)
                layernorm(1)
                scale_u(2)
                select_scores(3)
                layernorm(2)
                gain_o(0)
                scale_u(3)
                layernorm(3)
                for h in range(1, HEADS):
                    gain_o(h)

                def scale_g(h):
                    acc_at(N_G + h + 1)
                    dve.tensor_tensor(g[h], acc[h][:, :], rstdT[:, :], ALU.mult).then_inc(g_lin, 1)

                def mix(h):
                    side_wait(f"mix{h}")
                    dve.tensor_tensor(mt[h].rearrange("p (c i) -> p c i", c=CH),
                                      side(f"mix{h}")[:, :].rearrange("p (c i) -> p c i", c=CH),
                                      spatial_b_sb[:, h * P:(h + 1) * P].unsqueeze(1).broadcast_to([P, CH, P]),
                                      ALU.add).then_inc(mixed, 1)
                    dve.wait_ge(mixed, L * 4 + (h + 1))
                    dve.wait_ge(u_gelu, L * 4 + (h + 1))
                    dve.tensor_tensor(mt[h], mt[h], u[:, h * S:(h + 1) * S], ALU.mult).then_inc(u_mixed, 1)

                def lo_of(src, k):
                    dve.wait_ge(feat_hi_done, L * NF + (k + 1))
                    dve.tensor_tensor(featT(False, k), src, featT(True, k).bitcast(F32),
                                      ALU.subtract).then_inc(feat_ready, 1)

                def diagonal_o(h):
                    for part in range(2):
                        a = part * 16 + h * CH
                        dve.tensor_tensor(odiag[part][h].rearrange("p (c i) -> p c i", c=CH),
                                          ident.unsqueeze(1).broadcast_to([P, CH, P]),
                                          o_rstd_parts[:, a:a + CH].bitcast(F32).unsqueeze(2)
                                          .broadcast_to([P, CH, P]), ALU.mult).then_inc(odiag_done, 1)

                def norm_o(h):
                    side_wait(f"ospread{h}")
                    dve.wait_ge(og_done, L * 4 + (h + 1))
                    dve.tensor_tensor(mt[h], A[h], side(f"ospread{h}")[:, :], ALU.mult).then_inc(o_normed, 1)
                    dve.wait_ge(o_normed, L * 4 + (h + 1))
                    dve.wait_ge(g_silu, L * 4 + (h + 1))
                    dve.tensor_tensor(mt[h], mt[h], g[h], ALU.mult).then_inc(o_gated, 1)

                scale_g(0)
                mix(0)
                mix(1)
                lo_of(mt[0], 0)
                lo_of(mt[1], 1)
                scale_g(1)
                dve.wait_ge(o_std_done, L + 1)
                dve.reciprocal(o_rstd[:, :], o_std[:, :]).then_inc(o_rstd_done, 1)
                dve.wait_ge(o_rstd_done, L * 3 + 1)
                dve.tensor_copy(o_rstd_parts[:, 0:16], o_rstd[:, :]).then_inc(o_rstd_done, 1)
                dve.wait_ge(o_rstd_done, L * 3 + 2)
                dve.tensor_tensor(o_rstd_parts[:, 16:32], o_rstd[:, :], o_rstd_parts[:, 0:16].bitcast(F32),
                                  ALU.subtract).then_inc(o_rstd_done, 1)
                dve.wait_ge(o_rstd_done, L * 3 + 3)
                mix(2)
                mix(3)
                dve.wait_ge(u_mixed, L * 4 + 4)
                diagonal_o(0)
                diagonal_o(1)
                lo_of(mt[2], 2)
                scale_g(2)
                norm_o(0)
                diagonal_o(2)
                diagonal_o(3)
                lo_of(mt[3], 3)
                lo_of(mt[0], 4)
                norm_o(1)
                scale_g(3)
                lo_of(mt[1], 5)
                norm_o(2)
                norm_o(3)
                lo_of(mt[2], 6)
                lo_of(mt[3], 7)

                def add_to_x(n, m, j):
                    dve.wait_ge(acc_ready, n + 1)
                    dve.tensor_tensor(x[:, bass.ds(m * S, S)], x[:, bass.ds(m * S, S)], acc[j][:, :],
                                      ALU.add).then_inc(x_done, 1)

                with dve.Fori(0, KT // RING) as q:
                    for j in range(RING):
                        m = q * RING + j
                        add_to_x(L * NS + m + N_OUT, m, j)
                        gain_lo(m, L * 2 + 1)
                        add_square(m, L * 2 + 1, j % 2)
                token_scale(L * 2 + 1)
                start_squares()
                for i in range(4):
                    for edge in (0, S + 1):
                        dve.memset(y[i][:, edge:edge + 1], 0.0).then_inc(halo, 1)
                dve.wait_ge(halo, L * 8 + 8)
                dve.wait_ge(rstdT_done, L * 2 + 2)
                on_its_own(dve)

                def up_quad(slab, tile, feat, feat_lo_of):
                    def low_part(b):
                        dve.wait_ge(feat_hi_done, L * NF + tile + (b + KT + 1))
                        dve.tensor_tensor(feat_lo_of(b), gated[b], feat(b).bitcast(F32),
                                          ALU.subtract).then_inc(feat_ready, 1)

                    for b in range(2):
                        f = L * FT + tile + b
                        for v in range(2):
                            j = 2 * b + v
                            coef = (f * 2 + v) * 4
                            dve.wait_ge(acc_ready, L * NS + slab + (j + 1))
                            dve.tensor_tensor(y[j][:, 1:S + 1], acc[j][:, :], rstdT[:, :],
                                              ALU.mult).then_inc(y_ready, 1)
                            if b == 1 and v == 0:
                                low_part(0)
                            dve.wait_ge(centre_done, f * 2 + v + 1)
                            for tap in (0, 2):
                                dve.scalar_tensor_tensor(out=z[j], in0=y[j][:, tap:tap + S],
                                                         scalar=conv_sb[:, bass.ds(coef + tap, 1)], in1=z[j],
                                                         op0=ALU.mult, op1=ALU.add).then_inc(taps_done, 1)
                                dve.wait_ge(taps_done, f * 4 + (2 * v + tap // 2 + 1))
                        dve.wait_ge(silu_done, f + 1)
                        dve.tensor_tensor(gated[b], z[2 * b], z[2 * b + 1], ALU.mult).then_inc(gated_done, 1)
                    low_part(1)

                with dve.Fori(0, FULL_PARTS) as part:
                    for half, hi, lo in ((0, feat_hi, feat_lo), (1, feat2_hi, feat2_lo)):
                        with dve.Fori(0, 2) as q:
                            up_quad(part * PART + q * RING + (N_FFN + half * 8), part * KT + q * 2 + half * 4,
                                    lambda b: hi[:, bass.ds(q * (2 * S) + b * S, S)],
                                    lambda b: lo[:, bass.ds(q * (2 * S) + b * S, S)])
                    with dve.Fori(0, KT // RING) as q:
                        for j in range(RING):
                            add_to_x(L * NS + part * PART + q * RING + (N_FFN + 2 * KT + j), q * RING + j, j)
                for q in range(LAST_TILES // 2):
                    up_quad(N_LAST + q * RING, FULL_PARTS * KT + 2 * q, lambda b: featT(True, 2 * q + b),
                            lambda b: featT(False, 2 * q + b))
                with dve.Fori(0, KT // RING) as q:
                    for j in range(RING):
                        m = q * RING + j
                        add_to_x(L * NS + m + (N_LAST + 2 * LAST_TILES), m, j)
                        add_square(m, L * 2 + 2, j % 2)
                        with dve.If(L < DEPTH - 1):
                            gain_lo(m, L * 2 + 2)

            token_scale_on_partitions(DEPTH)
            dve.wait_ge(rstd_done, DEPTH + 1)
            dve.tensor_tensor(diag.rearrange("p (c i) -> p c i", c=CH),
                              ident.unsqueeze(1).broadcast_to([P, CH, P]),
                              rstd[:, :].unsqueeze(2).broadcast_to([P, CH, P]), ALU.mult).then_inc(diag_done, 1)
            dve.wait_ge(side_ready, DEPTH * NSIDE + 2)
            for m in range(KT):
                col = 2 * DEPTH * KT + m
                dve.scalar_tensor_tensor(out=xg_out(m), in0=x[:, m * S:(m + 1) * S],
                                         scalar=gains_sb[:, col:col + 1], in1=side("spread")[:, :],
                                         op0=ALU.mult, op1=ALU.mult).then_inc(final_done, 1)

        @block.tensor
        def _(pe):
            def three(out, w_pair, a_pair, first, last):
                (wh, wl), (ah, al) = w_pair, a_pair
                pe.matmul(out, wh, ah, start=first, stop=False)
                pe.matmul(out, wh, al, start=False, stop=False)
                return pe.matmul(out, wl, ah, start=False, stop=last)

            def w_block(j, at, n=P):
                a = j * SLAB + at
                return w_hi[:, a:a + n], w_lo[:, a:a + n]

            def xg(k, a=0, n=S):
                return xg_hi[:, k * S + a:k * S + a + n], xg_lo[:, k * S + a:k * S + a + n]

            def feat(k):
                return featT(True, k), featT(False, k)

            def project(j, source, blocks=KT, ready=None):
                for k in range(blocks):
                    if ready is not None:
                        pe.wait_ge(ready[0], ready[1] + (k + 1))
                    last = three(acc[j][:, :], w_block(j, k * P), source(k), k == 0, k == blocks - 1)
                last.then_inc(acc_ready, 1)

            def project_pair(source, blocks, ready):
                early = blocks - 2
                for k, j in ([(k, j) for j in range(2) for k in range(early)]
                             + [(k, j) for k in range(early, blocks) for j in range(2)]):
                    if j == 0:
                        pe.wait_ge(ready[0], ready[1] + (k + 1))
                    last = three(acc[j][:, :], w_block(j, k * P), source(k), k == 0, k == blocks - 1)
                    if k == blocks - 1:
                        last.then_inc(acc_ready, 1)

            def token_sums(name, r):
                pe.wait_ge(ssq_added, (r + 1) * (KT + 1))
                for c in range(CH):
                    last = pe.matmul(side(name)[:, c:c + 1], ssq[:, c * P:(c + 1) * P], ones[:, 0:1],
                                     start=True, stop=True)
                last.then_inc(side_ready, 1)

            def keep_busy(products):
                for _ in range(products):
                    pe.matmul(side_banks[3][:, 0:P], ones, ones, start=True, stop=True)

            def spread(name, d):
                pe.matmul(side(name)[:, :], ones[:, :], d, start=True, stop=True).then_inc(side_ready, 1)

            pe.wait_ge(ones_set, 1)
            with pe.Fori(0, 6):
                keep_busy(4)
            pe.wait_ge(setup_done, 2)

            with pe.Fori(0, DEPTH) as L:
                def slab_wait(n):
                    pe.wait_ge(lo_done, L * NS + (n + 1 + RING))

                for tiles in ((0, 1, 2, 3), (4, 5), (6,), (7,)):
                    for j in range(2):
                        if tiles[0] == 0:
                            pe.wait_ge(hi_done, L * NS + (j + 1))
                            pe.wait_ge(x_done, L * NX + (j + 1))
                        for k in tiles:
                            if j == 0:
                                pe.wait_ge(xg_ready, L * 16 + (k + 1))
                            w = w_block(j, k * P)[0]
                            pe.matmul(acc[j][:, :], w, xg(k)[0], start=(k == 0), stop=False)
                            pe.matmul(acc[j][:, :], w, xg(k)[1], start=False, stop=False)
                    for j in range(2):
                        if tiles[0] == 0:
                            slab_wait(j)
                        for k in tiles:
                            last = pe.matmul(acc[j][:, :], w_block(j, k * P)[1], xg(k)[0],
                                             start=False, stop=(k == KT - 1))
                        if tiles[-1] == KT - 1:
                            last.then_inc(acc_ready, 1)
                pe.wait_ge(rank_lo_done, L + 1)
                for k in range(KT):
                    for part in range(2):
                        last = pe.matmul(side("rankT")[:, :], rank_split[:, k * 4 * RANK:k * 4 * RANK + P],
                                         xg(k)[part], start=(k == 0 and part == 0), stop=(k == KT - 1 and part == 1))
                last.then_inc(side_ready, 1)
                pe.wait_ge(ssq_added, (L * 2 + 1) * (KT + 1))
                spread("spread", ssq[:, :])
                token_sums("sum", L * 2)
                slab_wait(2)
                project(2, xg)
                pe.wait_ge(rankT_done, L + 1)
                pe.wait_ge(par_loaded, L * 64 + 64)
                for t in range(CH):
                    pe.matmul(side(f"z{t}")[:, :], rankT[:, t * P:(t + 1) * P], gate_sb[:, :],
                              start=True, stop=True).then_inc(side_ready, 1)

                slab_wait(3)
                project(3, xg)

                def token_major(n0, s, bank_free=None):
                    slab_wait(n0 + s)
                    for kk in range(2):
                        k = 2 * s + kk
                        for t in range(CH):
                            if k == 0:
                                pe.wait_ge(*bank_free(t))
                            (wh, wl), (ah, al) = w_block(s, kk * S, S), xg(k, t * P, P)
                            pe.matmul(acc[t][:, :], ah, wh, start=(k == 0), stop=False)
                            pe.matmul(acc[t][:, :], al, wh, start=False, stop=False)
                            last = pe.matmul(acc[t][:, :], ah, wl, start=False, stop=(k == KT - 1))
                            if k == KT - 1:
                                last.then_inc(acc_ready, 1)
                    if s < 3:
                        last.then_inc(group_used, 1)

                def vb_bank(t):
                    return (kT_done, L * 2 + (t + 1)) if t < 2 else (qT_done, L * 2 + (t - 1))

                token_major(N_VB, 0, vb_bank)
                token_major(N_VB, 1, vb_bank)
                for dt in range(4):
                    pe.wait_ge(la_done, L * 4 + 4)
                    for c in range(CH):
                        last = pe.matmul(side(f"cum{dt}")[:, c * P:(c + 1) * P], la[c][:, dt * P:(dt + 1) * P],
                                         upto if dt < 2 else since, start=True, stop=True)
                    last.then_inc(side_ready, 1)
                token_major(N_VB, 2)
                token_major(N_VB, 3)
                token_major(N_VA, 0, lambda t: (vb_done, L * 4 + (t + 1)))
                pe.wait_ge(keT_done, L * 4 + 4)
                for c in range(CH):
                    for t in range(4):
                        last = pe.transpose(side(f"keys{c}")[:, t * P:(t + 1) * P], keT[t][:, c * P:(c + 1) * P],
                                            ident)
                    last.then_inc(side_ready, 1)
                token_major(N_VA, 1)
                for s in range(3):
                    pe.wait_ge(kend_done, L * 4 + 4)
                    for d, c in ((0, s), (1, CH - 1 - s)):
                        for h in range(HEADS):
                            a = (h % 2) * DK
                            last = pe.matmul(side(f"state{s}")[a:a + DK, (2 * d + h // 2) * P:(2 * d + h // 2 + 1) * P],
                                             kend[c][:, d * 256 + h * DK:d * 256 + (h + 1) * DK],
                                             vb[c][:, h * P:(h + 1) * P], start=True, stop=True)
                    last.then_inc(side_ready, 1)
                token_major(N_VA, 2)
                token_major(N_VA, 3)

                def scores(h):
                    a, pair = (h % 2) * DK, h // 2
                    for d, name in ((0, f"score_f{h}"), (1, f"score_b{h}")):
                        pe.wait_ge(*score_bank[name])
                        for c in range(CH):
                            w = slice(c * P, (c + 1) * P)
                            last = pe.matmul(side(name)[:, w], ki[2 * d + pair][a:a + DK, w],
                                             qd[2 * d + pair][a:a + DK, w], start=True, stop=True)
                        last.then_inc(side_ready, 1)

                score_bank = {
                    "score_f0": (kend_done, L * 4 + 4), "score_b0": (state_done, L * 9 + 1),
                    "score_f1": (state_done, L * 9 + 5), "score_b1": (state_done, L * 9 + 9),
                    "score_f2": (score_copied, L * 4 + 1), "score_b2": (score_done, L * 4 + 1),
                    "score_f3": (score_copied, L * 4 + 2), "score_b3": (score_done, L * 4 + 2)}

                def o_head(h):
                    a, pair = (h % 2) * DK, h // 2
                    pe.wait_ge(*((score_copied, L * 4 + 3), (score_done, L * 4 + 3),
                                 (score_copied, L * 4 + 4), (score_done, L * 4 + 4))[h])
                    pe.wait_ge(score_done, L * 4 + (h + 1))
                    for c in range(CH):
                        w = slice(c * P, (c + 1) * P)
                        out = side(f"o{h}")[:, w]
                        last = pe.matmul(out, vb[c][:, h * P:(h + 1) * P], A[h][:, w], start=True, stop=False)
                        if c > 0:
                            last = pe.matmul(out, state[a:a + DK, c - 1, 0, pair, :], qd[pair][a:a + DK, w],
                                             start=False, stop=(c == CH - 1))
                        if c < CH - 1:
                            last = pe.matmul(out, state[a:a + DK, 2 - c, 1, pair, :], qd[2 + pair][a:a + DK, w],
                                             start=False, stop=True)
                    last.then_inc(side_ready, 1)

                def mix(h):
                    for c in range(CH):
                        last = pe.matmul(side(f"mix{h}")[:, c * P:(c + 1) * P], va[:, (c * 4 + h) * P:(c * 4 + h + 1) * P],
                                         spatial_sb[:, h * P:(h + 1) * P], start=True, stop=True)
                    last.then_inc(side_ready, 1)

                def project_and_sum_o(j):
                    for k in range(KT):
                        last = three(acc[j][:, :], w_block(j, k * P), xg(k), k == 0, k == KT - 1)
                        if k == 0:
                            pe.wait_ge(osq_done, L * 4 + 4)
                            pe.wait_ge(og_done, L * 4 + 3)
                        for i in (2 * k, 2 * k + 1):
                            last_sum = pe.matmul(side("osum")[:, i:i + 1],
                                                 osq[i // 4][:, (i % 4) * P:(i % 4 + 1) * P],
                                                 ones[:, 0:1], start=True, stop=True)
                    last.then_inc(acc_ready, 1)
                    last_sum.then_inc(side_ready, 1)

                for h in range(HEADS):
                    slab_wait(N_U + h)
                    pe.wait_ge(va_gelu, L * 4 + (h + 1))
                    project(h, xg)
                    if h == 0:
                        pe.wait_ge(qk_done, L * 8 + 8)
                        scores(0)
                    elif h == 1:
                        scores(1)
                        scores(2)
                    elif h == 2:
                        scores(3)
                        o_head(0)
                    else:
                        o_head(1)
                        o_head(2)
                        o_head(3)
                for h in range(HEADS):
                    slab_wait(N_G + h)
                    pe.wait_ge(u_lin, L * 4 + (h + 1))
                    if h == 1:
                        project_and_sum_o(h)
                    else:
                        project(h, xg)
                    if h == 0:
                        pe.wait_ge(vn_done, L * 8 + 8)
                        pe.wait_ge(og_done, L * 4 + 1)
                        mix(0)
                        pe.wait_ge(og_done, L * 4 + 2)
                        mix(1)
                    elif h == 1:
                        pe.wait_ge(og_done, L * 4 + 4)
                        mix(2)
                        pe.wait_ge(mixed, L * 4 + 1)
                        mix(3)
                    else:
                        for i in (0, 1) if h == 2 else (2, 3):
                            pe.wait_ge(odiag_done, L * 8 + 2 * (i + 1))
                            pe.wait_ge(*((mixed, L * 4 + 2), (o_std_done, L + 1),
                                         (mixed, L * 4 + 3), (mixed, L * 4 + 4))[i])
                            for part in range(2):
                                last = pe.matmul(side(f"ospread{i}")[:, :], ones_r[:, :], odiag[part][i],
                                                 start=(part == 0), stop=(part == 1))
                            last.then_inc(side_ready, 1)
                with pe.Fori(0, KT // RING) as q:
                    for j in (1, 2, 3):
                        pe.wait_ge(lo_done, L * NS + q * RING + (N_OUT + j + 1 + RING))
                        pe.wait_ge(g_lin, L * 4 + (j + 1))
                        pe.wait_ge(x_done, L * NX + q * (j + 1) + RING)
                        if j == 1:
                            project_pair(feat, KT, (feat_ready, L * NF))
                        else:
                            project(j, feat)
                def up_first(slab, x_before, with_scale):
                    for j in range(RING):
                        slab_wait(slab + j)
                        pe.wait_ge(x_done, L * NX + (x_before + RING + j + 1 + RING))
                        project(j, xg, ready=(xg_ready, L * 16 + KT) if with_scale and j == 0 else None)
                        if with_scale and j == 0:
                            pe.wait_ge(o_normed, L * 4 + 3)
                            pe.wait_ge(ssq_added, (L * 2 + 2) * (KT + 1))
                            spread("ffn_spread", ssq[:, :])

                def up_rest(slab, y_before, quads):
                    with pe.Fori(1, quads) as q:
                        for j in range(RING):
                            pe.wait_ge(lo_done, L * NS + q * RING + (slab + j + 1 + RING))
                            pe.wait_ge(y_ready, L * NY + q * RING + (y_before + j + 1 - RING))
                            project(j, xg)

                def down(slab, x_before, y_before, blocks, feats):
                    with pe.Fori(0, KT // RING) as q:
                        for j in (1, 2, 3):
                            pe.wait_ge(lo_done, L * NS + q * RING + (slab + j + 1 + RING))
                            pe.wait_ge(y_ready, L * NY + (y_before + j + 1))
                            pe.wait_ge(x_done, L * NX + q * (j + 1) + (x_before + RING))
                            if j == 1:
                                project_pair(feat, blocks, (feat_ready, L * NF + feats))
                            else:
                                project(j, feat, blocks)

                for part in range(FULL_PARTS + 1):
                    tiles = KT if part < FULL_PARTS else LAST_TILES
                    slab = N_FFN + part * PART
                    up_first(slab, part * KT, part == 0)
                    up_rest(slab, part * 2 * KT, tiles // 2)
                    down(slab + 2 * tiles, (part + 1) * KT, part * 2 * KT + 2 * tiles - RING, tiles,
                         (part + 1) * KT)

            keep_busy(12)
            token_sums("sum", 2 * DEPTH)
            keep_busy(6)
            pe.wait_ge(diag_done, 1)
            spread("spread", diag)


def kernel(x, g_mix, w_in, w_s, b_s, ln_g, ln_b, w_gate_f, b_gate_f, w_gate_b, b_gate_b,
           g_gla, w_out, g_ffn, w_up, conv_w, conv_b, w_down, g_final):
    import numpy as np
    import concourse.bacc as bacc
    from concourse.bass_utils import run_bass_kernel_spmd

    ins = [np.asarray(a) for a in (x, g_mix, w_in, w_s, b_s, ln_g, ln_b, w_gate_f, b_gate_f, w_gate_b, b_gate_b,
                                   g_gla, w_out, g_ffn, w_up, conv_w, conv_b, w_down, g_final)]
    (x, g_mix, w_in, w_s, b_s, ln_g, ln_b, w_gate_f, b_gate_f, w_gate_b, b_gate_b,
     g_gla, w_out, g_ffn, w_up, conv_w, conv_b, w_down, g_final) = ins
    f32 = np.float32

    def channel_major(w, rows, col):
        t = len(rows) // P
        out = np.zeros((P, SLAB), f32)
        out[:, :t * P] = w[rows.start:rows.stop, col:col + P].reshape(t, P, P).transpose(1, 0, 2).reshape(P, t * P)
        return out

    def token_major(w, s, col):
        return w[2 * s * P:2 * (s + 1) * P, col:col + S].reshape(2, P, S).transpose(1, 0, 2).reshape(P, SLAB)

    A_W = B_W = 512
    QK = HEADS * DK
    U, VA, Q, K, VB, G = 0, A_W, 2 * A_W, 2 * A_W + QK, 2 * A_W + 2 * QK, 2 * A_W + 2 * QK + B_W
    R = G + B_W
    every = range(0, D)
    slabs = []
    for l in range(DEPTH):
        slabs += [channel_major(w_in[l], every, c) for c in (K, K + P, Q, Q + P)]
        slabs += [token_major(w_in[l], s, VB) for s in range(4)]
        slabs += [token_major(w_in[l], s, VA) for s in range(4)]
        slabs += [channel_major(w_in[l], every, U + h * P) for h in range(4)]
        slabs += [channel_major(w_in[l], every, G + h * P) for h in range(4)]
        slabs += [channel_major(w_out[l], every, m * P) for m in range(KT)]
        for first in range(0, FT, KT):
            tiles = range(first, min(first + KT, FT))
            for f in tiles:
                slabs += [channel_major(w_up[l], every, f * P), channel_major(w_up[l], every, DFF + f * P)]
            rows = range(tiles.start * P, tiles.stop * P)
            slabs += [channel_major(w_down[l], rows, m * P) for m in range(KT)]
    slabs = np.stack(slabs)
    gate = np.zeros((DEPTH, 4 * RANK + 1, 2 * QK), f32)
    for rows in (0, 2 * RANK):
        gate[:, rows:rows + RANK, :QK] = w_gate_f
        gate[:, rows + RANK:rows + 2 * RANK, QK:] = w_gate_b
    gate[:, 4 * RANK, :QK] = b_gate_f
    gate[:, 4 * RANK, QK:] = b_gate_b
    gains = np.stack([g_mix[0], g_ffn[0], g_mix[1], g_ffn[1], g_final])
    j, i = np.arange(P)[:, None], np.arange(P)[None, :]
    arrays = {
        "xT": x[0].T,
        "slabs": slabs,
        "rank_w": w_in[:, :, R:].reshape(DEPTH, KT, P, 2 * RANK).transpose(2, 0, 1, 3).reshape(P, -1),
        "gate_w": gate,
        "spatial_w": w_s.transpose(0, 3, 1, 2).reshape(DEPTH, P, HEADS * P),
        "spatial_b": b_s.reshape(DEPTH, HEADS * P),
        "ln_gb": np.concatenate([ln_g.reshape(DEPTH, -1), ln_b.reshape(DEPTH, -1)], 1),
        "gains": gains.reshape(2 * DEPTH + 1, KT, P).transpose(2, 0, 1).reshape(P, -1),
        "gla_gain": g_gla.reshape(DEPTH * HEADS, P).T,
        "conv": np.concatenate([conv_w, conv_b[:, None]], 1).reshape(DEPTH, 4, 2, FT, P)
                  .transpose(4, 0, 3, 2, 1).reshape(P, -1),
        "consts": np.concatenate([j == i, j <= i, j >= i, j > i], 1).astype(f32),
    }
    arrays = {n: np.ascontiguousarray(a) for n, a in arrays.items()}
    nc = bacc.Bacc("TRN2", target_bir_lowering=False, num_devices=1)
    args = [nc.dram_tensor(n, a.shape, F32, kind="ExternalInput").ap() for n, a in arrays.items()]
    args.append(nc.dram_tensor("outT", (D, S), F32, kind="ExternalOutput").ap())
    encoder(nc, *args)
    r = run_bass_kernel_spmd(nc, [arrays], core_ids=[0])
    return np.ascontiguousarray(r.results[0]["outT"].T)[None]
```
